# Optimizing a Trainium2 kernel written in Bass

```python
import jax, jax.numpy as jnp
from jax import lax
import numpy as np

D_MODEL = 1024
BATCH = 1
SEQ = 1024
DEPTH = 2
DEC_BATCH = 1
DEC_SEQ = 32
PAST_LEN = 128

CHUNK = 64
N_META = 16
MIX_W = D_MODEL
ATTN_W = MIX_W // 2
LRU_W = MIX_W - ATTN_W
V_DIM = 64
N_HEADS = ATTN_W // V_DIM
QK_NOPE = 64
QK_ROPE = 32
Q_LORA = 768
KV_LORA = 256
LRU_BLOCKS = 8
LRU_BW = LRU_W // LRU_BLOCKS
LRU_C = 8.0
CONV_W = 4
D_FF = 4 * D_MODEL
ROPE_THETA = 10000.0
Q_BLOCK = 128
EPS = 1e-6
SM_SCALE = (QK_NOPE + QK_ROPE) ** -0.5
IN_SPLITS = (Q_LORA, Q_LORA + KV_LORA, Q_LORA + KV_LORA + QK_ROPE, Q_LORA + KV_LORA + QK_ROPE + LRU_W)
IN_W = Q_LORA + KV_LORA + QK_ROPE + 2 * LRU_W

kernel_name = "hybrid_streaming_mla_rglru_step"

def rmsnorm(x, g):
    xf = x.astype(jnp.float32)
    y = xf * lax.rsqrt(jnp.mean(xf * xf, axis=-1, keepdims=True) + EPS)
    return (y * g.astype(jnp.float32)).astype(x.dtype)

def rope(x, pos):
    inv = ROPE_THETA ** (-jnp.arange(0, QK_ROPE, 2, dtype=jnp.float32) / QK_ROPE)
    ang = pos.astype(jnp.float32)[:, None] * inv[None, :]
    cos, sin = jnp.cos(ang), jnp.sin(ang)
    if x.ndim == 4:
        cos, sin = cos[:, None, :], sin[:, None, :]
    x1, x2 = jnp.split(x.astype(jnp.float32), 2, axis=-1)
    return jnp.concatenate([x1 * cos - x2 * sin, x1 * sin + x2 * cos], axis=-1).astype(x.dtype)

def expand_rows(rows, b):
    return jnp.broadcast_to(rows, (b,) + rows.shape[1:])

def lru_combine(left, right):
    a1, b1 = left
    a2, b2 = right
    return a1 * a2, a2 * b1 + b2

def mixer_project(x, pos, h0, conv_buf, p):
    B, T, _ = x.shape
    z = rmsnorm(x, p["norm_mix_g"]) @ p["w_in"]
    c_q, c_kv, k_r, x_r, g_r = jnp.split(z, IN_SPLITS, axis=-1)
    q = (rmsnorm(c_q, p["q_norm_g"]) @ p["w_uq"]).reshape(B, T, N_HEADS, QK_NOPE + QK_ROPE)
    q_nope = q[..., :QK_NOPE]
    q_pe = rope(q[..., QK_NOPE:], pos)
    ckv = rmsnorm(c_kv, p["kv_norm_g"])
    kpe = rope(k_r, pos)
    xpad = jnp.concatenate([expand_rows(conv_buf, B).astype(x.dtype), x_r], axis=1)
    xc = p["conv_b"] + sum(xpad[:, k:k + T] * p["conv_w"][k] for k in range(CONV_W))
    new_buf = xpad[:, T:]
    xb = xc.reshape(B, T, LRU_BLOCKS, LRU_BW)
    r = jax.nn.sigmoid(jnp.einsum("btnc,ncd->btnd", xb, p["w_gate_a"]).reshape(B, T, LRU_W) + p["b_gate_a"])
    i = jax.nn.sigmoid(jnp.einsum("btnc,ncd->btnd", xb, p["w_gate_x"]).reshape(B, T, LRU_W) + p["b_gate_x"])
    log_a = -LRU_C * r.astype(jnp.float32) * jax.nn.softplus(-p["lru_lambda"].astype(jnp.float32))
    a = jnp.exp(log_a)
    b = jnp.sqrt(-jnp.expm1(2.0 * log_a)) * (i * xc).astype(jnp.float32)
    b = b.at[:, 0].add(a[:, 0] * expand_rows(h0, B).astype(jnp.float32))
    _, h = lax.associative_scan(lru_combine, (a, b), axis=1)
    y = h.astype(x.dtype) * jax.nn.gelu(g_r)
    return q_nope, q_pe, ckv, kpe, y, h[:, -1].astype(x.dtype), new_buf

def attend_block(q_nope, q_pe, q_chunk, k_nope, k_pe, v, k_chunk):
    s = jnp.einsum("bqhd,bkhd->bhqk", q_nope, k_nope) + jnp.einsum("bqhr,bkr->bhqk", q_pe, k_pe)
    s = s.astype(jnp.float32) * SM_SCALE
    mask = k_chunk[None, :] <= q_chunk[:, None]
    s = jnp.where(mask[None, None], s, -1e30)
    w = jax.nn.softmax(s, axis=-1).astype(v.dtype)
    return jnp.einsum("bhqk,bkhd->bqhd", w, v)

def chunk_causal_attention(q_nope, q_pe, q_chunk, k_nope, k_pe, v, k_chunk):
    B, T = q_nope.shape[0], q_nope.shape[1]
    if T <= Q_BLOCK or T % Q_BLOCK != 0:
        return attend_block(q_nope, q_pe, q_chunk, k_nope, k_pe, v, k_chunk)
    nb = T // Q_BLOCK
    qn = q_nope.reshape(B, nb, Q_BLOCK, N_HEADS, QK_NOPE).swapaxes(0, 1)
    qp = q_pe.reshape(B, nb, Q_BLOCK, N_HEADS, QK_ROPE).swapaxes(0, 1)
    qc = q_chunk.reshape(nb, Q_BLOCK)

    def one_block(args):
        bn, bp, bc = args
        return attend_block(bn, bp, bc, k_nope, k_pe, v, k_chunk)

    o = lax.map(one_block, (qn, qp, qc))
    return o.swapaxes(0, 1).reshape(B, T, N_HEADS, V_DIM)

def layer_output(x, q_nope, q_pe, pos, ckv_keys, kpe_keys, key_pos, y_lru, p):
    B, T, _ = x.shape
    kv = jnp.einsum("bkc,chd->bkhd", ckv_keys, p["w_ukv"].reshape(KV_LORA, N_HEADS, QK_NOPE + V_DIM))
    k_nope, v = kv[..., :QK_NOPE], kv[..., QK_NOPE:]
    o = chunk_causal_attention(q_nope, q_pe, jnp.floor_divide(pos, CHUNK), k_nope, kpe_keys, v,
                               jnp.floor_divide(key_pos, CHUNK))
    merged = jnp.concatenate([rmsnorm(o.reshape(B, T, ATTN_W), p["attn_out_g"]),
                              rmsnorm(y_lru, p["lru_out_g"])], axis=-1)
    h = x + merged @ p["w_out"]
    f = jnp.square(jax.nn.relu(rmsnorm(h, p["norm_mlp_g"]) @ p["w_up"])) @ p["w_down"]
    return h + f

def setup_inputs(seed: int = 0) -> dict:
    key = jax.random.key(seed)
    ks = jax.random.split(key, 27)
    f32 = jnp.float32

    def nrm(k, shape, scale):
        return jax.random.normal(k, shape, f32) * scale

    def gain(k, shape):
        return 1.0 + 0.02 * jax.random.normal(k, shape, f32)

    u = jax.random.uniform(ks[19], (DEPTH, LRU_W), f32, 0.9, 0.999)
    return {
        "x_prompt": nrm(ks[0], (BATCH, SEQ, D_MODEL), 1.0),
        "x_sample": nrm(ks[1], (DEC_BATCH, DEC_SEQ, D_MODEL), 1.0),
        "cache_ckv": nrm(ks[2], (DEPTH, DEC_BATCH, PAST_LEN, KV_LORA), 1.0),
        "cache_kpe": nrm(ks[3], (DEPTH, DEC_BATCH, PAST_LEN, QK_ROPE), 1.0),
        "state_lru_h": nrm(ks[4], (DEPTH, DEC_BATCH, LRU_W), 0.5),
        "state_conv": nrm(ks[5], (DEPTH, DEC_BATCH, CONV_W - 1, LRU_W), 1.0),
        "meta_tokens": nrm(ks[6], (N_META, D_MODEL), 1.0),
        "norm_mix_g": gain(ks[7], (DEPTH, D_MODEL)),
        "w_in": nrm(ks[8], (DEPTH, D_MODEL, IN_W), D_MODEL ** -0.5),
        "q_norm_g": gain(ks[9], (DEPTH, Q_LORA)),
        "w_uq": nrm(ks[10], (DEPTH, Q_LORA, N_HEADS * (QK_NOPE + QK_ROPE)), Q_LORA ** -0.5),
        "kv_norm_g": gain(ks[11], (DEPTH, KV_LORA)),
        "w_ukv": nrm(ks[12], (DEPTH, KV_LORA, N_HEADS * (QK_NOPE + V_DIM)), KV_LORA ** -0.5),
        "conv_w": nrm(ks[13], (DEPTH, CONV_W, LRU_W), CONV_W ** -0.5),
        "conv_b": nrm(ks[14], (DEPTH, LRU_W), 0.02),
        "w_gate_a": nrm(ks[15], (DEPTH, LRU_BLOCKS, LRU_BW, LRU_BW), LRU_BW ** -0.5),
        "b_gate_a": nrm(ks[16], (DEPTH, LRU_W), 0.02),
        "w_gate_x": nrm(ks[17], (DEPTH, LRU_BLOCKS, LRU_BW, LRU_BW), LRU_BW ** -0.5),
        "b_gate_x": nrm(ks[18], (DEPTH, LRU_W), 0.02),
        "lru_lambda": jnp.log(u) - jnp.log1p(-u),
        "attn_out_g": gain(ks[20], (DEPTH, ATTN_W)),
        "lru_out_g": gain(ks[21], (DEPTH, LRU_W)),
        "w_out": nrm(ks[22], (DEPTH, MIX_W, D_MODEL), MIX_W ** -0.5),
        "norm_mlp_g": gain(ks[23], (DEPTH, D_MODEL)),
        "w_up": nrm(ks[24], (DEPTH, D_MODEL, D_FF), D_MODEL ** -0.5),
        "w_down": nrm(ks[25], (DEPTH, D_FF, D_MODEL), D_FF ** -0.5),
        "final_norm_g": gain(ks[26], (D_MODEL,)),
    }

def reference(x_prompt, x_sample, cache_ckv, cache_kpe, state_lru_h, state_conv, meta_tokens,
              norm_mix_g, w_in, q_norm_g, w_uq, kv_norm_g, w_ukv, conv_w, conv_b,
              w_gate_a, b_gate_a, w_gate_x, b_gate_x, lru_lambda, attn_out_g, lru_out_g,
              w_out, norm_mlp_g, w_up, w_down, final_norm_g):
    dt = x_prompt.dtype
    b_p, seq = x_prompt.shape[0], x_prompt.shape[1]
    b_s, dec_seq = x_sample.shape[0], x_sample.shape[1]
    past_len = cache_ckv.shape[2]
    meta_pos = jnp.arange(-N_META, 0, dtype=jnp.int32)
    prompt_pos = jnp.arange(seq, dtype=jnp.int32)
    sample_pos = past_len + jnp.arange(dec_seq, dtype=jnp.int32)
    prompt_key_pos = jnp.concatenate([meta_pos, prompt_pos])
    sample_key_pos = jnp.concatenate([meta_pos, jnp.arange(past_len, dtype=jnp.int32), sample_pos])

    h_meta = meta_tokens[None].astype(dt)
    h_p, h_s = x_prompt, x_sample
    ckv_p_l, kpe_p_l, lru_p_l, conv_p_l = [], [], [], []
    ckv_s_l, kpe_s_l, lru_s_l, conv_s_l = [], [], [], []
    for l in range(DEPTH):
        p = {"norm_mix_g": norm_mix_g[l], "w_in": w_in[l], "q_norm_g": q_norm_g[l], "w_uq": w_uq[l],
             "kv_norm_g": kv_norm_g[l], "w_ukv": w_ukv[l], "conv_w": conv_w[l], "conv_b": conv_b[l],
             "w_gate_a": w_gate_a[l], "b_gate_a": b_gate_a[l], "w_gate_x": w_gate_x[l],
             "b_gate_x": b_gate_x[l], "lru_lambda": lru_lambda[l], "attn_out_g": attn_out_g[l],
             "lru_out_g": lru_out_g[l], "w_out": w_out[l], "norm_mlp_g": norm_mlp_g[l],
             "w_up": w_up[l], "w_down": w_down[l]}
        mq_n, mq_p, m_ckv, m_kpe, m_y, m_h, m_buf = mixer_project(
            h_meta, meta_pos, jnp.zeros((1, LRU_W), dt), jnp.zeros((1, CONV_W - 1, LRU_W), dt), p)
        pq_n, pq_p, p_ckv, p_kpe, p_y, p_h, p_buf = mixer_project(h_p, prompt_pos, m_h, m_buf, p)
        h_p = layer_output(h_p, pq_n, pq_p, prompt_pos,
                           jnp.concatenate([expand_rows(m_ckv, b_p), p_ckv], axis=1),
                           jnp.concatenate([expand_rows(m_kpe, b_p), p_kpe], axis=1),
                           prompt_key_pos, p_y, p)
        sq_n, sq_p, s_ckv, s_kpe, s_y, s_h, s_buf = mixer_project(h_s, sample_pos, state_lru_h[l], state_conv[l], p)
        h_s = layer_output(h_s, sq_n, sq_p, sample_pos,
                           jnp.concatenate([expand_rows(m_ckv, b_s), cache_ckv[l].astype(dt), s_ckv], axis=1),
                           jnp.concatenate([expand_rows(m_kpe, b_s), cache_kpe[l].astype(dt), s_kpe], axis=1),
                           sample_key_pos, s_y, p)
        if l + 1 < DEPTH:
            h_meta = layer_output(h_meta, mq_n, mq_p, meta_pos, m_ckv, m_kpe, meta_pos, m_y, p)
        ckv_p_l.append(p_ckv); kpe_p_l.append(p_kpe); lru_p_l.append(p_h); conv_p_l.append(p_buf)
        ckv_s_l.append(s_ckv); kpe_s_l.append(s_kpe); lru_s_l.append(s_h); conv_s_l.append(s_buf)

    y_prompt = rmsnorm(h_p, final_norm_g)
    y_sample = rmsnorm(h_s, final_norm_g)
    new_ckv_prompt = jnp.stack(ckv_p_l)
    new_kpe_prompt = jnp.stack(kpe_p_l)
    new_lru_h_prompt = jnp.stack(lru_p_l)
    new_conv_prompt = jnp.stack(conv_p_l)
    new_ckv_sample = jnp.stack(ckv_s_l)
    new_kpe_sample = jnp.stack(kpe_s_l)
    new_lru_h_sample = jnp.stack(lru_s_l)
    new_conv_sample = jnp.stack(conv_s_l)
    return (y_prompt, y_sample, new_ckv_prompt, new_kpe_prompt, new_lru_h_prompt, new_conv_prompt,
            new_ckv_sample, new_kpe_sample, new_lru_h_sample, new_conv_sample)


_drawn_inputs = setup_inputs


def setup_inputs(seed=0):
    import zlib

    import numpy as np

    out = dict(_drawn_inputs(seed))
    spreads = {}
    factors = {'q_norm_g': 4.24,
     'b_gate_a': 8.0,
     'b_gate_x': 5.473,
     'attn_out_g': 11.875,
     'lru_out_g': 11.527,
     'norm_mlp_g': 2.893,
     'final_norm_g': 7.96}
    for name, (base, spread) in spreads.items():
        noise = np.random.default_rng([zlib.crc32(name.encode()), seed]).standard_normal(out[name].shape)
        drawn = base * np.exp(spread * noise) if base else spread * noise
        out[name] = __import__('jax').numpy.asarray(drawn.astype(out[name].dtype))
    for name, factor in factors.items():
        out[name] = (out[name] * factor).astype(out[name].dtype)
    return out
```

```python
from contextlib import ExitStack

import numpy as np
import concourse.bass as bass
from concourse import mybir

F32 = mybir.dt.float32
F32R = mybir.dt.float32r
ALU = mybir.AluOpType
ACT = mybir.ActivationFunctionType
AX_X = mybir.AxisListType.X

P = 128
DM, SEQ, DEPTH, DEC, PAST = 1024, 1024, 2, 32, 128
NMETA, QL, KVL, ROPE, NOPE, NH, LRU, ATT, CW, DFF = 16, 768, 256, 32, 64, 8, 512, 512, 4, 4096
VD = 64
EPS = 1e-6
SM_SCALE = float((NOPE + ROPE) ** -0.5)
STREAM = NMETA + SEQ
TOK = STREAM + DEC
T = TOK + 2
CH = T // 3
KW = 1296
KCH = KW // 3
PAST_A, META2, PAST_B, KEY_END = TOK, TOK + 96, TOK + 96 + NMETA, TOK + 96 + NMETA + 32
GELU_C = float(np.sqrt(2.0 / np.pi))

B_XR, B_GR, B_CKV, B_KR = [0, 1, 2, 3], [5, 6, 8, 9], [11, 12], 14
B_GATE = [4, 7, 10, 13]
B_CQ = [15, 16, 17, 18, 19, 20]
B_UQ, B_UV, B_UK = 21, 27, 28
B_OY, B_OO, B_MLP = 29, 34, 38
GROUPS, GT = 4, 8
NB = B_MLP + GROUPS * 2 * GT

U_SMIX = 0
U_XR, U_GATE, U_GR, U_CKV = [1, 2, 3, 4], [5, 9, 13, 17], [7, 8, 11, 12], [15, 16]
U_KR, U_SKV, U_SQ = 19, 21, 28
U_CQ = [20, 22, 23, 24, 25, 26]
U_UQ = [27, 29, 30, 31, 32, 33]
U_SY, U_V, U_K = 34, 35, 45
U_OY, U_SO, U_OO, U_SMLP, U_MLP = [49, 50, 51, 52, 54, 55, 56, 57], 53, 58, 66, 67
NU = U_MLP + GROUPS * 2 * GT

READ = {U_SMIX: ("root", 1), U_KR: ("kr_ev", 1), U_SKV: ("root", 2), U_SQ: ("root", 3), U_SY: ("root", 4), U_SO: ("root", 5), U_SMLP: ("root", 6)}
for _c in range(4):
    READ[U_XR[_c]] = ("xr_ev", _c + 1)
    READ[U_GR[_c]] = ("gr_ev", _c + 1)
    READ[U_GATE[_c]] = ("gate_r", _c + 1)
    READ[U_GATE[_c] + 1] = ("gate_i", _c + 1)
    READ[U_UQ[_c]] = ("qn", _c + 1)
    READ[U_K + _c] = ("kf", _c + 1)
for _c in range(2):
    READ[U_CKV[_c]] = ("ckv_ev", _c + 1)
    READ[U_UQ[4 + _c]] = ("qr_ev", _c + 1)
for _c in range(6):
    READ[U_CQ[_c]] = ("cq_ev", _c + 1)
for _c in range(8):
    READ[U_OY[_c]] = ("oy_ev", _c + 1)
    READ[U_OO + _c] = ("res_add", _c + 1)
for _c in range(10):
    READ[U_V + _c] = ("v_lo", _c + 1)

LAST_UNIT = {}
for _c in range(4):
    LAST_UNIT[B_XR[_c]] = U_XR[_c]
    LAST_UNIT[B_GR[_c]] = U_GR[_c]
    LAST_UNIT[B_GATE[_c]] = U_GATE[_c] + 1
    LAST_UNIT[B_OO + _c] = U_OO + 2 * _c + 1
for _c in range(2):
    LAST_UNIT[B_CKV[_c]] = U_CKV[_c]
for _c in range(6):
    LAST_UNIT[B_CQ[_c]] = U_CQ[_c]
    LAST_UNIT[B_UQ + _c] = U_UQ[_c]
LAST_UNIT[B_KR], LAST_UNIT[B_UV], LAST_UNIT[B_UK] = U_KR, U_V + 9, U_K + 3
OY_TILES = [(0, 1), (2, 3), (4, 5), (6,), (7,)]
for _c, _m in enumerate(OY_TILES):
    LAST_UNIT[B_OY + _c] = U_OY[_m[-1]]
for _c in range(2 * GT * GROUPS):
    LAST_UNIT[B_MLP + _c] = U_MLP + _c

WCOLS = {b: 1024 for b in range(NB)}
for _c in range(4):
    WCOLS[B_GATE[_c]] = 256
for _c in range(6):
    WCOLS[B_UQ + _c] = 768
WCOLS[B_OY + 3] = WCOLS[B_OY + 4] = 512

V_GMIX, V_QG, V_KVG, V_CW, V_CB, V_BA, V_BX, V_LAM, V_AG, V_LG, V_MG, V_GNEXT = 0, 8, 14, 16, 32, 36, 40, 44, 48, 52, 56, 64
NVEC = 72

META_ROWS = NMETA
PAIRS = [(9, META2, META_ROWS, 0, 272, 0), (9, META2, META_ROWS, 272, 384, 0), (9, META2, META_ROWS, 656, 384, 0)]
for _t in range(8):
    _q = NMETA + 128 * _t
    for _lo, _hi in ((0, 272), (272, 656), (656, STREAM)):
        if _hi > _q:
            _q0 = max(_q, _lo)
            PAIRS.append((_t, NMETA + 128 * _t, P, _q0, _hi - _q0, 1 if _q0 == _q else 0))
SAMPLE_PAIRS = [(8, STREAM, P, STREAM, DEC, 0), (9, META2, NMETA + 32, STREAM, DEC, 0)]
PAIRS = PAIRS + SAMPLE_PAIRS
NP = len(PAIRS)
LAG = 2
MX_FROM = 3
DVE_CHAIN = 82
VTILES = [NMETA + 128 * t for t in range(8)] + [STREAM, META2]
VW = 65 * NH


def o_place(q0):
    if q0 >= STREAM:
        return 5, 272 + q0 - STREAM
    if q0 < 272:
        return 5, q0
    return (6, q0 - 272) if q0 < 656 else (7, q0 - 656)


def group(q0):
    return 3 if q0 >= STREAM else 0 if q0 < 272 else 1 if q0 < 656 else 2


FIRST = [min(i for i, x in enumerate(PAIRS) if group(x[3]) == g) for g in range(4)]
LAST = [max(i for i, x in enumerate(PAIRS) if group(x[3]) == g) for g in range(4)]

MAXES = []
for _t in range(7):
    _n = NMETA + 128 * (_t + 1)
    _b = [(0, 0, max(256, min(_n, 512)))] + ([(1, 512 if _n - 512 > 64 else _n - 256, max(256, _n - 512))] if _n > 512 else [])
    if _t == 3:
        _r = [(0, P, 0, _n - 64, 0, 3), (64, P, 512 + 192, 64, 1, 3)]
    else:
        _r = [(0, P, 0, _n - 64, 0, _t), (64, P, _n - 64, 64, 1, _t)]
    MAXES.append((NMETA + 128 * _t, _b, _r))
MAXES.append((NMETA + 896, [(0, 0, 512), (1, 512, 464)], [(0, P, 0, 976, 0, 7)]))
MAXES.append((NMETA + 896, [(0, 784, 256)], [(64, P, 192, 64, 1, 7)]))
MAXES.append((0, [(0, 0, 256)], [(0, NMETA, 0, NMETA, 0, 8)]))
MAXES.append((TOK - P, [(0, STREAM, 256)], [(96, P, 0, KEY_END - STREAM, 0, 9)]))
NMX = len(MAXES)


def last_use(n, i, key):
    for j in range(i - 1, -1, -1):
        if key(j) == key(i):
            return j
    return None


def trunk(nc, xT, wst, vec, fgain, ropeC, ropeS, ident_in, past_ckv, past_kpe, h0, conv0,
          yT, ckv_out, kpe_out, h_out, conv_out, x_scr, sum_scr):
    ctx = ExitStack()
    with ctx:
        enter = ctx.enter_context

        TB, KB = T * 4, KW * 4
        total = 6 * 4096 + 8 * TB + 16 * TB + 8 * TB + 64 + 4 * TB + 2 * KB + KB + 2 * TB + TB
        base = -(-nc.sbuf_base // 32) * 32
        enter(nc.sbuf_tensor("arena", [P, (total + 64) // 4], F32))
        regions = {}
        at = base
        for name, size in (("W", 6 * 4096), ("X", 8 * TB), ("R", 16 * TB), ("F", 8 * TB + 64), ("G", 4 * TB),
                           ("CK", 2 * KB), ("KP", KB), ("CS", 2 * TB), ("RS", TB)):
            regions[name] = at
            at += size

        def place(name, region, offset, cols, dt=F32):
            return nc.alloc_sbuf_tensor_at(name, [P, cols], dt, offset=regions[region] + offset, align_bytes=8)

        def tiles(name, region, first, n, dt=F32):
            return [place(f"{name}{i}", region, (first + i) * TB, T, dt) for i in range(n)]

        raw = [place(f"raw{i}", "W", i * 4096, 1024) for i in range(2)]
        whi = [place(f"whi{i}", "W", (2 + i) * 4096, 1024, F32R) for i in range(2)]
        wlo = [place(f"wlo{i}", "W", (4 + i) * 4096, 1024, F32R) for i in range(2)]
        xall = place("xall", "F", 0, 8 * T)
        x = [xall[:, m * T:(m + 1) * T] for m in range(8)]
        xgh, xgl = tiles("xgh", "R", 8, 8, F32R), tiles("xgl", "R", 0, 8, F32R)
        xc = tiles("xc", "F", 0, 4)
        t1, t2, t3 = tiles("t", "F", 4, 3)
        t4 = place("t4", "F", 7 * TB, T + 16)
        g = tiles("g", "G", 0, 4)
        ckv = [place(f"ckv{i}", "CK", i * KB, KW) for i in range(2)]
        kpe = place("kpe", "KP", 0, KW)
        cosT, sinT = tiles("rope", "CS", 0, 2)
        cq = tiles("cq", "X", 0, 6)
        xch, xcl = tiles("xcs", "X", 6, 2, F32R)
        sqa, sqt = tiles("sqa", "X", 6, 2)
        rs = place("rs", "RS", 0, T)
        cqh, cql = tiles("cqh", "R", 0, 6, F32R), tiles("cql", "R", 8, 6, F32R)
        ckvh = [place("ckvh0", "R", 6 * TB, KW, F32R), place("ckvh1", "R", 14 * TB, KW, F32R)]
        ckvl = [place(f"ckvl{i}", "CK", i * KB, KW, F32R) for i in range(2)]
        qn, qr = tiles("qn", "X", 0, 4), tiles("qr", "X", 4, 2)
        rtmp = place("rtmp", "X", 6 * TB, T)
        kf = [place(f"kf{i}", "R", 8 * TB + i * KB, KW) for i in range(4)]
        ra = [place(f"ra{i}", "F", 20992 + i * TB, T) for i in range(3)] + [place("ra3", "R", 20992, T)]
        vh, vl = place("vh", "F", 0, 10 * VW, F32R), place("vl", "R", 0, 10 * VW, F32R)
        qs = [[place("qeh", "R", 6 * TB, T, F32R), place("qel", "R", 7 * TB, T, F32R)],
              [place("qoh", "CS", 0, T, F32R), place("qol", "CS", TB, T, F32R)]]
        ke = 8 * TB + 4 * KB
        ks = [[place("keh", "R", ke, KW, F32R), place("kel", "R", ke + KB, KW, F32R)],
              [place("koh", "CK", 0, KW, F32R), place("kol", "CK", KB, KW, F32R)]]
        pd = [place(f"pd{i}", "X", 4 * TB + 1536 * i, 384) for i in range(2)]
        pn = [place(f"pn{i}", "X", 4 * TB + 1536 * (2 + i), 384) for i in range(2)]
        ph = [place(f"ph{i}", "X", 4 * TB + 1536 * (4 + i), 384, F32R) for i in range(2)]
        pl = [place(f"pl{i}", "X", 4 * TB + 1536 * (6 + i), 384, F32R) for i in range(2)]
        ph.append(place("ph2", "R", ke + 2 * KB, 384, F32R))
        pl.append(place("pl2", "R", ke + 2 * KB + 1536, 384, F32R))
        rc = place("rc", "X", 4 * TB + 1536 * 8, T)
        srow = place("srow", "KP", 0, T)
        o = tiles("o", "X", 0, 4)
        yh = tiles("yh", "R", 8, 4, F32R)
        yl = tiles("yl", "R", 12, 4, F32R)
        oh, ol = tiles("oh", "X", 4, 4, F32R), tiles("ol", "X", 0, 4, F32R)
        osq = place("osq", "CK", 0, T)
        osqt = place("osqt", "CK", TB, T)
        msq = place("msq", "CS", TB, T)
        xmh, xml = tiles("xmh", "R", 8, 8, F32R), tiles("xml", "R", 0, 8, F32R)
        fh, fl = tiles("fh", "X", 0, 8, F32R), tiles("fl", "G", 0, 8, F32R)

        def sb(name, shape, dt=F32):
            return enter(nc.sbuf_tensor(name, shape, dt))

        vecs = sb("vecs", [P, NVEC])
        fg = sb("fg", [P, 8])
        half_ba, half_bx = sb("half_ba", [P, 4]), sb("half_bx", [P, 4])
        sp2, spw = sb("sp2", [P, 4]), sb("spw", [P, 16])
        eps = sb("eps", [P, 1])
        ones = sb("ones", [P, P])
        ident = sb("ident", [P, P])
        past = sb("past", [P, 2, PAST])
        xs = sb("xs", [P, 4, CW - 1 + DEC + 2])
        cbuf = sb("cbuf", [P, 4, 2, CW - 1])
        hbuf = sb("hbuf", [P, 4, 2])
        h0s = sb("h0s", [P, 4])
        mx, mx2 = sb("mx", [P, P]), sb("mx2", [P, 8])
        mth, mtl = sb("mth", [16, P], F32R), sb("mtl", [16, P], F32R)
        comp = nc.alloc_sbuf_tensor_at("comp", [16, 2 * TOK // 16], F32, offset=regions["KP"] + TB, align_bytes=8)
        ps = enter(nc.psum_tensor("ps", [P, 8, 512], F32))

        PER = {}

        def sem(name, per_layer=0):
            s = enter(nc.semaphore(name))
            PER[name] = per_layer
            S[name] = s

        S = {}
        for name, per in (
            ("dve_chain", DVE_CHAIN), ("raw0", 16 * NB // 2), ("raw1", 16 * NB // 2), ("w_hi", NB), ("w_lo", NB), ("mm", NU),
            ("vec_in", 64), ("table_in", 32), ("const_in", 0), ("const_set", 0),
            *((f"x_in{m}", 16) for m in range(8)), ("x_load", 0), ("x_out", 16 * 8), ("xg_hi", 8), ("xg_lo", 8), ("sq", 8), ("sq_sum", 7),
            ("root", 6), ("rstd", 6),
            ("xr_ev", 4), ("conv", 4), ("xc_hi", 4), ("xc_lo", 4),
            ("gate_r", 4), ("gate_t", 4), ("gate_i", 4), ("root_t", 4), ("lru_w", 4), ("hid", 4),
            ("gr_ev", 4), ("g_sq", 4), ("g_cube", 4), ("g_tanh", 4), ("y", 4),
            ("ckv_ev", 2), ("ckv_sq", 2), ("ckv_sum", 1), ("ckv_n", 2), ("ckv_hi", 2), ("ckv_lo", 2),
            ("kr_ev", 1), ("kpe_new", 1), ("kpe_meta", 1), ("kpe", 16 * 8), ("kpe_out", 16), ("kv_out", 32), ("ckv_full", 1), ("hid_out", 1), ("small_out", 32), ("g_poly", 4), ("spw_abs", 1), ("spw_exp", 1), ("sp2", 1),
            ("cq_ev", 6), ("cq_sq", 6), ("cq_sum", 5), ("cq_hi", 6), ("cq_lo", 6),
            ("qn", 4), ("qr_ev", 2), ("qr", 2), ("ra", 16 * 8),
            ("y_sq", 4), ("y_sum", 3), ("y_n", 4), ("v_one", 1), ("v_hi", 10), ("v_lo", 10), ("kf", 4),
            ("kslot_hi", 2), ("kslot_lo", 2),
            ("slot_const", 1), ("row_set", 10), ("q_zero", 3), ("q_hi", NH), ("q_lo", NH), ("s", NH * NP), ("p", NH * NP), ("p_hi", NH * NP), ("p_lo", NH * NP),
            ("pv", NH * NP), ("mxmm", NH * NMX), ("mxred", NH * NMX), ("mxc", NH), ("mxt", NH), ("mt_hi", NH), ("mt_lo", NH),
            ("aug", 16 * 6 * NH), ("o_ev", NH), ("s_ev", NH), ("sum_out", 16 * NH), ("sum_in", 16 * 4), ("inv", 4), ("inv_out", 16 * 4),
            ("inv_in", 16 * NH), ("o", 4), ("o_sq", 4), ("o_sum", 3), ("o_n", 4), ("o_hi", 4), ("o_lo", 4),
            ("y_hi", 4), ("y_lo", 4), ("oy_ev", 8), ("xm_hi", 8), ("xm_lo", 8), ("xm_sq", 8), ("xm_sum", 7),
            ("relu", GROUPS * GT), ("f_sq", GROUPS * GT), ("f_hi", GROUPS * GT), ("f_lo", GROUPS * GT), ("res_add", 8 + GROUPS * 8),
            ("yout", 8), ("y_st", 0),
        ):
            sem(name, per)

        block = enter(nc.Block())

        def col(c):
            return vecs[:, c:c + 1]

        def chunks(tile):
            return tile[:, 0:T].rearrange("p (c n) -> p c n", c=3)

        def slot(u):
            return ps[:, 3 * (u % 2):3 * (u % 2) + 3, 0:CH]

        def half(e):
            return slice(64 * e, 64 * e + 64)

        def wait_alone(engine, name, value):
            value = engine.to_reg(value)
            engine.wait_ge(S["const_in"], 64)
            engine.wait_ge(S[name], value)

        PE_ROWS = [slice(64, 96), slice(0, 32)]
        SHIFT_ROW = [96, 32]
        MAX_ROWS, ALL_ROWS = [96, P], [97, P]

        @block.sync
        def _(sp):
            sp.dma_start(ones[:, :], ident_in[1]).then_inc(S["const_in"], 16)
            sp.dma_start(ident[:, :], ident_in[0]).then_inc(S["const_in"], 16)
            sp.dma_start(fg[:, :], fgain).then_inc(S["const_in"], 16)
            for m in range(8):
                sp.dma_start(x[m], xT[m]).then_inc(S["x_load"], 16)
            with sp.Fori(0, DEPTH) as L:
                def w(name, k):
                    assert k > 0, name
                    sp.wait_ge(S[name], L * PER[name] + k)

                for n in (0, 1):
                    sp.wait_ge(S["w_lo"], L * NB + 1)
                    sp.dma_start(raw[n][:, :], wst[L * NB + n]).then_inc(S[f"raw{n}"], 16)
                sp.wait_ge(S["xg_hi"], L * 8 + 8)
                sp.wait_ge(S["xg_lo"], L * 8 + 8)
                sp.dma_start(vecs[:, :], vec[L]).then_inc(S["vec_in"], 16)
                sp.dma_start(h0s[:, :], h0[L]).then_inc(S["vec_in"], 16)
                sp.dma_start(xs[:, :, 0:CW - 1], conv0[L]).then_inc(S["vec_in"], 16)
                sp.dma_start(past[:, :, :], past_ckv[L]).then_inc(S["vec_in"], 16)
                w("mm", U_SMIX + 1)
                sp.dma_start(cosT[:, :], ropeC).then_inc(S["table_in"], 16)
                sp.dma_start(sinT[:, :], ropeS).then_inc(S["table_in"], 16)
                with sp.Fori(1, 16) as i:
                    for n in (0, 1):
                        sp.wait_ge(S["w_lo"], L * NB + 2 * i + n)
                        sp.dma_start(raw[n][:, :], wst[L * NB + 2 * i + n]).then_inc(S[f"raw{n}"], 16)

                for h in range(NH):
                    if h in (0, 4):
                        w("qr", h // 4 + 1)
                    if h == 0:
                        w("y", 4)
                    src = qr[h // 4][32 * (h % 4):32 * (h % 4) + 32, :]
                    sp.dma_start(ra[h // 2][PE_ROWS[h % 2], :], src).then_inc(S["ra"], 16)

                for h in range(NH + 1):
                    if h < NH:
                        e = h % 2
                        r = slice(SHIFT_ROW[e], SHIFT_ROW[e] + 1)
                        w("mt_lo", h + 1)
                        for part, rows in ((0, mth), (1, mtl)):
                            q, m = qs[e][part][:, :].bitcast(F32), rows[:, :].bitcast(F32)
                            sp.dma_start(q[r, NMETA:STREAM].rearrange("a (t n) -> a t n", t=8), m[0:8, :]).then_inc(S["aug"], 16)
                            sp.dma_start(q[r, 0:NMETA], m[8:9, 0:NMETA]).then_inc(S["aug"], 16)
                            sp.dma_start(q[r, STREAM:TOK], m[9:10, P - DEC:P]).then_inc(S["aug"], 16)
                    if h >= 1:
                        k = h - 1
                        w("s_ev", k + 1)
                        sp.dma_start(sum_scr[k:k + 1, :], srow[64 * (k % 2):64 * (k % 2) + 1, 0:TOK]).then_inc(S["sum_out"], 16)
                        if k % 2 == 1:
                            j = k // 2
                            w("sum_out", 16 * (k + 1))
                            flat = sum_scr[2 * j:2 * j + 2, :].rearrange("a (r n) -> (a r) n", r=8)
                            sp.dma_start(comp[:, :], flat).then_inc(S["sum_in"], 16)
                            w("inv", j + 1)
                            sp.dma_start(flat, comp[:, :]).then_inc(S["inv_out"], 16)
                            w("inv_out", 16 * (j + 1))
                            for e in range(2):
                                sp.dma_start(rc[half(e), 0:TOK], sum_scr[2 * j + e:2 * j + e + 1, :].to_broadcast([64, TOK]))\
                                    .then_inc(S["inv_in"], 16)

                w("pv", NH * NP)
                for m in range(8):
                    sp.dma_start(x[m], x_scr[m]).then_inc(S[f"x_in{m}"], 16)
                with sp.Fori(16, NB // 2) as i:
                    for n in (0, 1):
                        sp.wait_ge(S["w_lo"], L * NB + 2 * i + n)
                        sp.dma_start(raw[n][:, :], wst[L * NB + 2 * i + n]).then_inc(S[f"raw{n}"], 16)
            for m in range(8):
                sp.wait_ge(S["yout"], m + 1)
                sp.dma_start(yT[m], x[m]).then_inc(S["y_st"], 16)
            sp.wait_ge(S["y_st"], 16 * 8)

        @block.tensor
        def _(pe):
            PASSES = (("h", "h"), ("h", "l"), ("l", "h"))

            with pe.Fori(0, DEPTH) as L:
                def w(name, k):
                    assert k > 0, name
                    pe.wait_ge(S[name], L * PER[name] + k)

                def take(u):
                    if u >= 2:
                        w(*READ[u - 2])

                def product(dst, u, b, woff, rhs_h, rhs_l, ready=None):
                    w("w_lo", b + 2)
                    take(u)
                    n = len(rhs_h)
                    for k in range(n):
                        if ready:
                            ready(k)
                        for i, (a, c) in enumerate(PASSES):
                            wt = (whi if a == "h" else wlo)[b % 2][:, woff + 128 * k:woff + 128 * k + 128]
                            r = (rhs_h if c == "h" else rhs_l)[k]
                            for q in range(3):
                                mm = nc.tensor.matmul(dst(q), wt, r(q), start=(k == 0 and i == 0), stop=(k == n - 1 and i == 2))
                    mm.then_inc(S["mm"], 1)

                def tok(tile):
                    return lambda q: tile[:, q * CH:(q + 1) * CH]

                def to_slot(u):
                    return lambda q: ps[:, 3 * (u % 2) + q, 0:CH]

                def norm_sum(u, tile):
                    take(u)
                    for q in range(3):
                        mm = nc.tensor.matmul(ps[:, 3 * (u % 2) + q, 0:CH], ones[:, :], tile[:, q * CH:(q + 1) * CH], start=True, stop=True)
                    mm.then_inc(S["mm"], 1)

                pe.wait_ge(S["const_in"], 64)
                pe.wait_ge(S["sq_sum"], L * 7 + 7)
                norm_sum(U_SMIX, msq)
                XH, XL = [tok(t) for t in xgh], [tok(t) for t in xgl]
                pe.wait_ge(S["xg_lo"], L * 8 + 8)

                def gates(c):
                    w("xc_lo", c + 1)
                    for k in range(2):
                        product(to_slot(U_GATE[c] + k), U_GATE[c] + k, B_GATE[c], 128 * k, [tok(xch)], [tok(xcl)])

                for c in range(4):
                    product(to_slot(U_XR[c]), U_XR[c], B_XR[c], 0, XH, XL)
                gates(0)
                for c in (0, 1):
                    product(to_slot(U_GR[c]), U_GR[c], B_GR[c], 0, XH, XL)
                gates(1)
                for c in (2, 3):
                    product(to_slot(U_GR[c]), U_GR[c], B_GR[c], 0, XH, XL)
                gates(2)
                for c in (0, 1):
                    product(to_slot(U_CKV[c]), U_CKV[c], B_CKV[c], 0, XH, XL)
                gates(3)
                product(to_slot(U_KR), U_KR, B_KR, 0, XH, XL)
                product(to_slot(U_CQ[0]), U_CQ[0], B_CQ[0], 0, XH, XL)
                w("ckv_sum", 1)
                norm_sum(U_SKV, sqa)
                for c in range(1, 6):
                    product(to_slot(U_CQ[c]), U_CQ[c], B_CQ[c], 0, XH, XL)
                for m in range(6):
                    product(to_slot(U_UQ[m]), U_UQ[m], B_UQ + m, 0, [tok(t) for t in cqh], [tok(t) for t in cql],
                            (lambda k: w("cq_lo", k + 1)) if m == 0 else None)
                    if m == 0:
                        w("cq_sum", 5)
                        norm_sum(U_SQ, sqa)
                w("y_sum", 3)
                norm_sum(U_SY, t3)
                w("w_lo", B_UV + 2)
                w("ckv_lo", 2)
                for t in range(10):
                    u = U_V + t
                    take(u)
                    c0 = VTILES[t]
                    for k in range(2):
                        for i, (a, c) in enumerate((("h", "h"), ("h", "l"), ("l", "h"))):
                            mm = nc.tensor.matmul(ps[:, 3 * (u % 2), :], (ckvh if a == "h" else ckvl)[k][:, c0:c0 + P],
                                                  (whi if c == "h" else wlo)[B_UV % 2][:, 512 * k:512 * k + 512],
                                                  start=(k == 0 and i == 0), stop=(k == 1 and i == 2))
                    mm.then_inc(S["mm"], 1)
                for j in range(4):
                    product(lambda q: ps[:, 3 * ((U_K + j) % 2) + q, 0:KCH], U_K + j, B_UK, 256 * j,
                            [(lambda q, t=t: t[:, q * KCH:(q + 1) * KCH]) for t in ckvh],
                            [(lambda q, t=t: t[:, q * KCH:(q + 1) * KCH]) for t in ckvl])

                take(U_K + 4)
                take(U_K + 5)

                def max_step(h, s):
                    e = h % 2
                    q0, banks, _ = MAXES[s]
                    rows = slice(0, MAX_ROWS[e])
                    if h or s:
                        w("mxred", h * NMX + s)
                    if s == 0:
                        w("q_hi", h + 1)
                        w("q_lo", h + 1)
                        if h % 2 == 1 and h >= 3:
                            w("q_zero", h // 2)
                        if h >= 1:
                            w("mxt", h)
                            w("mt_lo", h)
                    for bank, k0, n in banks:
                        mm = nc.tensor.matmul(ps[:, 3 + bank, 0:n], qs[e][0][rows, q0:q0 + P], ks[e][0][rows, k0:k0 + n], start=True, stop=True)
                    mm.then_inc(S["mxmm"], 1)

                def max_rows(h):
                    w("mxc", h + 1)
                    nc.tensor.transpose(ps[:, 3, 0:P], mx[:, :], ident[:, :]).then_inc(S["mxt"], 1)

                w("kslot_lo", 2)
                for s in range(NMX):
                    max_step(0, s)
                max_rows(0)
                for h in range(NH):
                    e = h % 2
                    rows = slice(0, ALL_ROWS[e])
                    for i in range(NP + LAG):
                        if i < NP:
                            gi = h * NP + i
                            _, k0, _, q0, n, _ = PAIRS[i]
                            if i == 0:
                                w("aug", 16 * 6 * (h + 1))
                            if gi >= 3:
                                w("p", gi - 2)
                            for j, (a, c) in enumerate(PASSES):
                                mm = nc.tensor.matmul(ps[:, gi % 3, 0:n], ks[e][0 if a == "h" else 1][rows, k0:k0 + P],
                                                      qs[e][0 if c == "h" else 1][rows, q0:q0 + n], start=(j == 0), stop=(j == 2))
                            mm.then_inc(S["s"], 1)
                        if h + 1 < NH:
                            if MX_FROM <= i < MX_FROM + NMX:
                                max_step(h + 1, i - MX_FROM)
                            if i == MX_FROM + NMX + 1:
                                max_rows(h + 1)
                        if i >= LAG:
                            k = i - LAG
                            gk = h * NP + k
                            kt, _, n_rows, q0, n, _ = PAIRS[k]
                            bank, c0 = o_place(q0)
                            w("p_lo", gk + 1)
                            if k == 0 and h >= 1:
                                w("o_ev", h)
                                w("s_ev", h)
                            v0 = VW * kt + 65 * h
                            for j, (v, p) in enumerate(((vh, ph), (vl, ph), (vh, pl))):
                                mm = nc.tensor.matmul(ps[0:65, bank, c0:c0 + n], v[0:n_rows, v0:v0 + 65], p[gk % 3][0:n_rows, 0:n],
                                                      start=(k in FIRST and j == 0), stop=(k in LAST and j == 2))
                            mm.then_inc(S["pv"], 1)

                w("o_ev", NH)
                w("s_ev", NH)
                w("mxt", NH)
                w("mt_lo", NH)
                for bi, ms in enumerate(OY_TILES):
                    for n, m in enumerate(ms):
                        if m == 4:
                            w("o_sum", 3)
                            norm_sum(U_SO, osq)
                        product(to_slot(U_OY[m]), U_OY[m], B_OY + bi, 512 * n, [tok(t) for t in yh], [tok(t) for t in yl],
                                (lambda k: w("y_lo", k + 1)) if m == 0 else None)
                for m in range(8):
                    product(to_slot(U_OO + m), U_OO + m, B_OO + m // 2, 512 * (m % 2), [tok(t) for t in oh], [tok(t) for t in ol],
                            (lambda k: w("o_lo", k + 1)) if m == 0 else None)

                w("xm_sum", 7)
                norm_sum(U_SMLP, msq)
                w("root", 6)
                wait_alone(pe, "res_add", L * PER["res_add"] + 8)
                w("xm_lo", 8)
                MH, ML = [tok(t) for t in xmh], [tok(t) for t in xml]
                FH, FL = [tok(t) for t in fh], [tok(t) for t in fl]
                with pe.Fori(0, GROUPS) as gg:
                    for k in range(2 * GT):
                        u, b = U_MLP + k, B_MLP + k
                        pe.wait_ge(S["w_lo"], L * NB + gg * (2 * GT) + (b + 2))
                        if k < 2:
                            pe.wait_ge(S["res_add"], L * PER["res_add"] + gg * 8 + (7 + k))
                        else:
                            name, j = ("relu", k - 1) if k < GT + 2 else ("res_add", 8 + k - 2 - GT + 1)
                            pe.wait_ge(S[name], L * PER[name] + gg * 8 + j)
                        rh, rl = (MH, ML) if k < GT else (FH, FL)
                        for kk in range(8):
                            if k == GT:
                                pe.wait_ge(S["f_lo"], L * PER["f_lo"] + gg * GT + (kk + 1))
                            for i, (a, c) in enumerate(PASSES):
                                wt = (whi if a == "h" else wlo)[b % 2][:, 128 * kk:128 * kk + 128]
                                for q in range(3):
                                    mm = nc.tensor.matmul(ps[:, 3 * (u % 2) + q, 0:CH], wt, (rh if c == "h" else rl)[kk](q),
                                                          start=(kk == 0 and i == 0), stop=(kk == 7 and i == 2))
                        mm.then_inc(S["mm"], 1)

            pe.wait_ge(S["sq_sum"], DEPTH * 7 + 7)
            pe.wait_ge(S["res_add"], DEPTH * PER["res_add"])
            for q in range(3):
                mm = nc.tensor.matmul(ps[:, q, 0:CH], ones[:, :], msq[:, q * CH:(q + 1) * CH], start=True, stop=True)
            mm.then_inc(S["mm"], 1)

        @block.scalar
        def _(act):
            act.dma_start(vecs[:, :], vec[0]).then_inc(S["const_in"], 16)
            act.wait_ge(S["const_in"], 64)
            act.wait_ge(S["x_load"], 128)
            for m in range(8):
                nc.scalar.activation(xgh[m][:, :], x[m], ACT.Copy, scale=col(V_GMIX + m)).then_inc(S["xg_hi"], 1)
                if m >= 2:
                    act.wait_ge(S["sq_sum"], m - 1)
                nc.scalar.activation((rs if m else msq)[:, :], x[m], ACT.Square).then_inc(S["sq"], 1)
            act.wait_ge(S["const_set"], 1)
            with act.Fori(0, DEPTH) as L:
                def w(name, k):
                    assert k > 0, name
                    act.wait_ge(S[name], L * PER[name] + k)

                def split(b):
                    w(f"raw{b % 2}", 16 * (b // 2 + 1))
                    if b >= 2:
                        w("mm", LAST_UNIT[b - 2] + 1)
                    n = WCOLS[b]
                    nc.scalar.activation(whi[b % 2][:, 0:n], raw[b % 2][:, 0:n], ACT.Copy).then_inc(S["w_hi"], 1)

                def root(u, dst, dim):
                    w("mm", u + 1)
                    nc.scalar.activation(chunks(dst), slot(u), ACT.Sqrt, scale=1.0 / dim, bias=eps[:, 0:1]).then_inc(S["root"], 1)

                def xc_hi(c):
                    w("conv", c + 1)
                    if c:
                        w("mm", U_GATE[c - 1] + 2)
                    nc.scalar.activation(xch[:, :], xc[c][:, :], ACT.Copy).then_inc(S["xc_hi"], 1)

                def gates(c):
                    w("mm", U_GATE[c] + 1)
                    if c:
                        w("hid", c)
                    else:
                        w("conv", 4)
                    nc.scalar.activation(chunks(t1), slot(U_GATE[c]), ACT.Tanh, scale=0.5, bias=half_ba[:, c:c + 1]).then_inc(S["gate_r"], 1)
                    w("gate_r", c + 1)
                    nc.scalar.activation(t1[:, :], t1[:, :], ACT.Tanh, scale=sp2[:, c:c + 1], bias=sp2[:, c:c + 1]).then_inc(S["gate_t"], 1)
                    w("mm", U_GATE[c] + 2)
                    nc.scalar.activation(chunks(t4), slot(U_GATE[c] + 1), ACT.Tanh, scale=0.5, bias=half_bx[:, c:c + 1]).then_inc(S["gate_i"], 1)
                    w("gate_t", c + 1)
                    nc.scalar.activation(t3[:, :], t1[:, :], ACT.Sqrt).then_inc(S["root_t"], 1)

                def gelu_a(c):
                    w("gr_ev", c + 1)
                    w("lru_w", c + 1)
                    nc.scalar.activation(t2[:, :], g[c][:, :], ACT.Square).then_inc(S["g_sq"], 1)

                def gelu_b(c):
                    w("g_cube", c + 1)
                    nc.scalar.activation(t2[:, :], t2[:, :], ACT.Tanh, scale=GELU_C).then_inc(S["g_tanh"], 1)

                split(0)
                root(U_SMIX, rs, DM)
                split(1)
                w("vec_in", 64)
                w("spw_abs", 1)
                nc.scalar.activation(spw[:, 4:8], spw[:, 0:4], ACT.Exp, scale=-1.0).then_inc(S["spw_exp"], 1)
                split(2)
                split(3)
                xc_hi(0)
                w("sp2", 1)
                for b in (4, 5, 6):
                    split(b)
                gates(0)
                xc_hi(1)
                split(7)
                gelu_a(0)
                split(8)
                gelu_b(0)
                split(9)
                gates(1)
                xc_hi(2)
                split(10)
                gelu_a(1)
                split(11)
                gelu_b(1)
                split(12)
                gates(2)
                xc_hi(3)
                split(13)
                gelu_a(2)
                split(14)
                gelu_b(2)
                split(15)
                gates(3)
                split(16)
                gelu_a(3)
                w("mm", U_GATE[3] + 2)
                for c in range(2):
                    w("ckv_ev", c + 1)
                    nc.scalar.activation((sqt if c else sqa)[:, :], ckv[c][:, 0:T], ACT.Square).then_inc(S["ckv_sq"], 1)
                gelu_b(3)
                split(17)
                root(U_SKV, sqt, KVL)

                def cq_square(c):
                    w("cq_ev", c + 1)
                    if c == 1:
                        w("ckv_n", 2)
                    if c >= 2:
                        w("cq_sum", c - 1)
                    nc.scalar.activation((sqt if c else sqa)[:, :], cq[c][:, :], ACT.Square).then_inc(S["cq_sq"], 1)

                cq_square(0)
                split(18)
                cq_square(1)
                split(19)
                cq_square(2)
                cq_square(3)
                split(20)
                cq_square(4)
                split(21)
                w("mm", U_CQ[5] + 1)
                for c in range(6):
                    if c == 1:
                        cq_square(5)
                    nc.scalar.activation(cqh[c][:, :], cq[c][:, :], ACT.Copy, scale=col(V_QG + c)).then_inc(S["cq_hi"], 1)
                split(22)
                w("ckv_full", 1)
                for c in range(2):
                    nc.scalar.activation(ckvh[c][:, :], ckv[c][:, :], ACT.Copy).then_inc(S["ckv_hi"], 1)
                w("cq_ev", 6)
                root(U_SQ, rs, QL)
                split(23)
                split(24)
                for c in range(4):
                    w("y", 4)
                    if c >= 2:
                        w("y_sum", c - 1)
                    nc.scalar.activation((t4[:, 0:T] if c else t3[:, :]), g[c][:, :], ACT.Square).then_inc(S["y_sq"], 1)
                for b in (25, 26, 27):
                    split(b)
                w("qr_ev", 2)
                root(U_SY, rs, LRU)
                split(28)
                w("v_one", 1)
                for t in range(10):
                    w("mm", U_V + t + 1)
                    dst = vh[:, VW * t:VW * (t + 1)].rearrange("p (h d) -> p h d", h=NH)[:, :, 0:64]
                    nc.scalar.activation(dst, ps[:, 3 * ((U_V + t) % 2), :].rearrange("p (h d) -> p h d", h=NH), ACT.Copy)\
                        .then_inc(S["v_hi"], 1)
                w("cq_lo", 6)
                for j in range(4):
                    w("mm", U_K + j + 1)
                    b0 = 3 * ((U_K + j) % 2)
                    nc.scalar.activation(kf[j][:, :].rearrange("p (c n) -> p c n", c=3), ps[:, b0:b0 + 3, 0:KCH], ACT.Copy).then_inc(S["kf"], 1)
                split(29)
                split(30)

                w("kpe", 16 * 8)
                w("slot_const", 1)
                for e in range(2):
                    nc.scalar.activation(ks[e][0][PE_ROWS[e], :], kpe[PE_ROWS[e], :], ACT.Copy).then_inc(S["kslot_hi"], 1)

                def load_hi(h):
                    j, e = h // 2, h % 2
                    if h == 0:
                        w("ra", 16 * NH)
                        w("qn", 4)
                        w("kf", 4)
                    if h >= 2:
                        w("s", (h - 1) * NP)
                    nc.scalar.activation(qs[e][0][half(e), :], qn[j][half(e), :], ACT.Copy)
                    nc.scalar.activation(qs[e][0][PE_ROWS[e], :], ra[j][PE_ROWS[e], :], ACT.Copy)
                    nc.scalar.activation(ks[e][0][half(e), :], kf[j][half(e), :], ACT.Copy).then_inc(S["q_hi"], 1)

                def shift_hi(h):
                    w("mxt", h + 1)
                    if h:
                        w("aug", 16 * 6 * h)
                    nc.scalar.activation(mth[0:10, :], ps[0:10, 3, 0:P], ACT.Copy, scale=-1.0).then_inc(S["mt_hi"], 1)

                def o_out(h):
                    w("pv", (h + 1) * NP)
                    d, r = o[h // 2], half(h % 2)
                    nc.scalar.activation(d[r, 0:272], ps[0:64, 5, 0:272], ACT.Copy)
                    nc.scalar.activation(d[r, STREAM:TOK], ps[0:64, 5, 272:272 + DEC], ACT.Copy)
                    nc.scalar.activation(d[r, 272:STREAM].rearrange("p (a n) -> p a n", a=2), ps[0:64, 6:8, 0:384], ACT.Copy).then_inc(S["o_ev"], 1)

                load_hi(0)
                shift_hi(0)
                w("row_set", 10)
                used = {"d": [], "n": []}
                for h in range(NH):
                    for i in range(NP):
                        gi = h * NP + i
                        _, _, rows, _, n, diag = PAIRS[i]
                        kind = "d" if diag else "n"
                        buf = (pd if diag else pn)[len(used[kind]) % 2]
                        w("s", gi + 1)
                        if len(used[kind]) >= 2:
                            w("p_lo", used[kind][-2] + 1)
                        used[kind].append(gi)
                        src = ps[:, gi % 3, :]
                        if diag:
                            nc.scalar.activation(buf[0:64, 0:64], src[0:64, 0:64], ACT.Exp, scale=SM_SCALE)
                            nc.scalar.activation(buf[:, 64:n], src[:, 64:n], ACT.Exp, scale=SM_SCALE).then_inc(S["p"], 1)
                        else:
                            nc.scalar.activation(buf[0:rows, 0:n], src[0:rows, 0:n], ACT.Exp, scale=SM_SCALE).then_inc(S["p"], 1)
                        if i == 0 and h >= 1:
                            o_out(h - 1)
                        if i == 1 and h + 1 < NH:
                            load_hi(h + 1)
                        if i == MX_FROM + NMX + 1 and h + 1 < NH:
                            shift_hi(h + 1)
                o_out(NH - 1)

                for c in range(4):
                    if c == 0:
                        w("y_n", 4)
                    nc.scalar.activation(yh[c][:, :], g[c][:, :], ACT.Copy, scale=col(V_LG + c)).then_inc(S["y_hi"], 1)
                split(31)
                for j in range(4):
                    w("o", j + 1)
                    if j >= 2:
                        w("o_sum", j - 1)
                    nc.scalar.activation((osqt if j else osq)[:, :], o[j][:, :], ACT.Square).then_inc(S["o_sq"], 1)
                    if j == 1:
                        split(32)
                root(U_SO, rs, ATT)
                split(33)
                for j in range(4):
                    w("o_n", j + 1)
                    nc.scalar.activation(oh[j][:, :], o[j][:, :], ACT.Copy, scale=col(V_AG + j)).then_inc(S["o_hi"], 1)
                split(34)
                split(35)
                for m in range(8):
                    if m and m % 2 == 0:
                        split(35 + m // 2)
                    w("res_add", m + 1)
                    nc.scalar.activation(xmh[m][:, :], x[m], ACT.Copy, scale=col(V_MG + m)).then_inc(S["xm_hi"], 1)
                    if m >= 2:
                        w("xm_sum", m - 1)
                    nc.scalar.activation((rs if m else msq)[:, :], x[m], ACT.Square).then_inc(S["xm_sq"], 1)
                split(B_MLP + 1)
                w("xm_sum", 7)
                root(U_SMLP, rs, DM)

                def mlp_group(gg, last):
                    for k in range(2 * GT):
                        if not (last and k >= 2 * GT - 2):
                            b = B_MLP + k + 2
                            act.wait_ge(S["mm"], L * NU + gg * (2 * GT) + (U_MLP + k + 1))
                            act.wait_ge(S[f"raw{b % 2}"], L * PER["raw0"] + gg * (16 * GT) + 16 * (b // 2 + 1))
                            nc.scalar.activation(whi[b % 2][:, :], raw[b % 2][:, :], ACT.Copy).then_inc(S["w_hi"], 1)
                        if k < GT:
                            act.wait_ge(S["relu"], L * PER["relu"] + gg * GT + (k + 1))
                            nc.scalar.activation(msq[:, :], msq[:, :], ACT.Square).then_inc(S["f_sq"], 1)
                            act.wait_ge(S["f_sq"], L * PER["f_sq"] + gg * GT + (k + 1))
                            nc.scalar.activation(fh[k][:, :], msq[:, :], ACT.Copy).then_inc(S["f_hi"], 1)
                        elif last:
                            m = k - GT
                            w("res_add", GROUPS * 8 + m + 1)
                            nc.scalar.activation(xgh[m][:, :], x[m], ACT.Copy, scale=col(V_GNEXT + m)).then_inc(S["xg_hi"], 1)
                            if m >= 2:
                                act.wait_ge(S["sq_sum"], L * 7 + 7 + (m - 1))
                            nc.scalar.activation((rs if m else msq)[:, :], x[m], ACT.Square).then_inc(S["sq"], 1)

                with act.Fori(0, GROUPS - 1) as gg:
                    mlp_group(gg, False)
                mlp_group(GROUPS - 1, True)
            act.wait_ge(S["mm"], DEPTH * NU + 1)
            act.wait_ge(S["sq_sum"], DEPTH * 7 + 7)
            nc.scalar.activation(chunks(rs), ps[:, 0:3, 0:CH], ACT.Sqrt, scale=1.0 / DM, bias=eps[:, 0:1]).then_inc(S["root"], 1)

        @block.vector
        def _(dve):
            V = nc.vector
            V.memset(eps[:, :], EPS).then_inc(S["w_lo"], 1)
            V.memset(mx[:, :], 0.0).then_inc(S["const_set"], 1)
            dve.wait_ge(S["const_in"], 64)
            for m in range(8):
                dve.wait_ge(S["xg_hi"], m + 1)
                V.scalar_tensor_tensor(out=xgl[m][:, :], in0=x[m], scalar=col(V_GMIX + m), in1=xgh[m][:, :].bitcast(F32),
                                       op0=ALU.mult, op1=ALU.subtract).then_inc(S["xg_lo"], 1)
            chain = [0]
            with dve.Fori(0, DEPTH) as L:
                def w(name, k):
                    assert k > 0, name
                    dve.wait_ge(S[name], L * PER[name] + k)

                def link(ins):
                    chain[0] += 1
                    ins.then_inc(S["dve_chain"], 1)
                    w("dve_chain", chain[0])

                def split(b):
                    w("w_hi", b + 1)
                    n = WCOLS[b]
                    V.tensor_tensor(wlo[b % 2][:, 0:n], raw[b % 2][:, 0:n], whi[b % 2][:, 0:n].bitcast(F32), ALU.subtract).then_inc(S["w_lo"], 1)

                def rstd(dst, n):
                    w("root", n)
                    V.reciprocal(dst[:, :], dst[:, :]).then_inc(S["rstd"], 1)
                    w("rstd", n)

                def scaled(u, dst, by, name):
                    w("mm", u + 1)
                    V.tensor_tensor(chunks(dst), slot(u), chunks(by), ALU.mult).then_inc(S[name], 1)

                def lo(dst, src, hi, name, gain=None):
                    if gain is None:
                        V.tensor_tensor(dst, src, hi.bitcast(F32), ALU.subtract).then_inc(S[name], 1)
                    else:
                        V.scalar_tensor_tensor(out=dst, in0=src, scalar=gain, in1=hi.bitcast(F32), op0=ALU.mult, op1=ALU.subtract)\
                            .then_inc(S[name], 1)

                def conv(c):
                    scaled(U_XR[c], t4[:, CW - 1:CW - 1 + T], rs, "xr_ev")
                    w("xr_ev", c + 1)
                    link(V.tensor_copy(xs[:, c, CW - 1:], t4[:, CW - 1 + STREAM:CW - 1 + T]))
                    V.tensor_copy(cbuf[:, c, 0, :], t4[:, STREAM:STREAM + CW - 1])
                    V.tensor_copy(cbuf[:, c, 1, :], t4[:, TOK:TOK + CW - 1])
                    for src, n, dst in ((t4[:, :], STREAM, xc[c][:, 0:STREAM]), (xs[:, c, :], DEC + 2, xc[c][:, STREAM:T])):
                        link(V.tensor_scalar(dst, src[:, 3:3 + n], col(V_CW + 4 * c + 3), col(V_CB + c), ALU.mult, ALU.add))
                        for k in (2, 1, 0):
                            ins = V.scalar_tensor_tensor(out=dst, in0=src[:, k:k + n], scalar=col(V_CW + 4 * c + k), in1=dst,
                                                         op0=ALU.mult, op1=ALU.add)
                            if k or n == STREAM:
                                link(ins)
                    ins.then_inc(S["conv"], 1)

                def xc_lo(c):
                    w("xc_hi", c + 1)
                    lo(xcl[:, :], xc[c][:, :], xch[:, :], "xc_lo")

                def lru(c):
                    w("gate_t", c + 1)
                    link(V.tensor_scalar(t2[:, :], t1[:, :], 1.0, None, ALU.add))
                    link(V.reciprocal(t2[:, :], t2[:, :]))
                    w("root_t", c + 1)
                    V.tensor_scalar(t1[:, :], t2[:, :], 2.0, -1.0, ALU.mult, ALU.add)
                    V.scalar_tensor_tensor(out=t3[:, :], in0=t3[:, :], scalar=2.0, in1=t2[:, :], op0=ALU.mult, op1=ALU.mult).then_inc(S["lru_w"], 1)
                    w("gate_i", c + 1)
                    link(V.scalar_tensor_tensor(out=t4[:, 0:T], in0=t4[:, 0:T], scalar=1.0, in1=xc[c][:, :], op0=ALU.add, op1=ALU.mult))
                    link(V.scalar_tensor_tensor(out=t4[:, 0:T], in0=t4[:, 0:T], scalar=0.5, in1=t3[:, :], op0=ALU.mult, op1=ALU.mult))
                    V.tensor_tensor_scan(xc[c][:, 0:STREAM], t1[:, 0:STREAM], t4[:, 0:STREAM], 0.0, ALU.mult, ALU.add)
                    V.tensor_tensor_scan(xc[c][:, STREAM:T], t1[:, STREAM:T], t4[:, STREAM:T], h0s[:, c:c + 1], ALU.mult, ALU.add)\
                        .then_inc(S["hid"], 1)
                    w("hid", c + 1)
                    V.tensor_copy(hbuf[:, c, 0:1], xc[c][:, STREAM - 1:STREAM])
                    link(V.tensor_copy(hbuf[:, c, 1:2], xc[c][:, TOK - 1:TOK]))

                def gelu(c):
                    w("g_tanh", c + 1)
                    link(V.scalar_tensor_tensor(out=g[c][:, :], in0=t2[:, :], scalar=1.0, in1=g[c][:, :], op0=ALU.add, op1=ALU.mult))
                    V.scalar_tensor_tensor(out=g[c][:, :], in0=g[c][:, :], scalar=0.5, in1=xc[c][:, :], op0=ALU.mult, op1=ALU.mult)\
                        .then_inc(S["y"], 1)

                HALF_SWAP = list(range(16, 32)) + list(range(16))

                def rotate(buf, tmp, name):
                    link(V.stream_shuffle(tmp, buf, HALF_SWAP))
                    link(V.tensor_tensor(tmp, tmp, sinT[:, :], ALU.mult))
                    link(V.tensor_tensor(buf, buf, cosT[:, :], ALU.mult))
                    V.tensor_tensor(buf, buf, tmp, ALU.add).then_inc(S[name], 1)

                split(0)
                rstd(rs, 1)
                split(1)
                w("vec_in", 64)
                lam = vecs[:, V_LAM:V_LAM + 4]
                V.tensor_scalar(half_ba[:, :], vecs[:, V_BA:V_BA + 4], 0.5, None, ALU.mult)
                V.tensor_scalar(half_bx[:, :], vecs[:, V_BX:V_BX + 4], 0.5, None, ALU.mult)
                link(V.tensor_scalar(sp2[:, :], lam, -1.0, 0.0, ALU.mult, ALU.max))
                V.scalar_tensor_tensor(out=spw[:, 0:4], in0=sp2[:, :], scalar=2.0, in1=lam, op0=ALU.mult, op1=ALU.add).then_inc(S["spw_abs"], 1)
                w("spw_exp", 1)
                e_, s_, s2, p_ = spw[:, 4:8], spw[:, 0:4], spw[:, 8:12], spw[:, 12:16]
                link(V.tensor_scalar(s2, e_, 2.0, None, ALU.add))
                link(V.reciprocal(s2, s2))
                link(V.tensor_tensor(s_, e_, s2, ALU.mult))
                link(V.tensor_tensor(s2, s_, s_, ALU.mult))
                link(V.tensor_scalar(p_, s2, 1.0 / 19, None, ALU.mult))
                for d in (17, 15, 13, 11, 9, 7, 5, 3):
                    link(V.scalar_tensor_tensor(out=p_, in0=p_, scalar=1.0 / d, in1=s2, op0=ALU.add, op1=ALU.mult))
                link(V.scalar_tensor_tensor(out=p_, in0=p_, scalar=1.0, in1=s_, op0=ALU.add, op1=ALU.mult))
                link(V.tensor_scalar(sp2[:, :], sp2[:, :], 2.0, None, ALU.mult))
                V.scalar_tensor_tensor(out=sp2[:, :], in0=p_, scalar=4.0, in1=sp2[:, :], op0=ALU.mult, op1=ALU.add).then_inc(S["sp2"], 1)

                dve.wait_ge(S["x_out"], L * 128 + 128)
                dve.wait_ge(S["sq"], L * 8 + 8)
                dve.wait_ge(S["xg_lo"], L * 8 + 8)
                link(V.memset(t4[:, 0:CW - 1], 0.0))
                conv(0)
                split(2)
                conv(1)
                split(3)
                xc_lo(0)
                conv(2)
                split(4)
                conv(3)
                split(5)
                split(6)
                xc_lo(1)
                lru(0)
                split(7)
                scaled(U_GR[0], g[0], rs, "gr_ev")
                split(8)
                scaled(U_GR[1], g[1], rs, "gr_ev")
                gelu(0)
                split(9)
                xc_lo(2)
                lru(1)
                split(10)
                scaled(U_GR[2], g[2], rs, "gr_ev")
                split(11)
                scaled(U_GR[3], g[3], rs, "gr_ev")
                gelu(1)
                split(12)
                xc_lo(3)
                lru(2)
                split(13)
                scaled(U_CKV[0], ckv[0][:, 0:T], rs, "ckv_ev")
                split(14)
                scaled(U_CKV[1], ckv[1][:, 0:T], rs, "ckv_ev")
                gelu(2)
                split(15)
                lru(3)
                scaled(U_KR, kpe[:, 0:T], rs, "kr_ev")
                split(16)
                scaled(U_CQ[0], cq[0], rs, "cq_ev")
                gelu(3)
                wait_alone(dve, "table_in", L * PER["table_in"] + 32)
                w("kr_ev", 1)
                rotate(kpe[:, 0:T], t1[:, :], "kpe_new")
                split(17)
                rstd(sqt, 2)
                for c in range(2):
                    V.scalar_tensor_tensor(out=ckv[c][:, 0:T], in0=ckv[c][:, 0:T], scalar=col(V_KVG + c), in1=sqt[:, :], op0=ALU.mult, op1=ALU.mult)\
                        .then_inc(S["ckv_n"], 1)
                w("ckv_n", 2)
                scaled(U_CQ[1], cq[1], rs, "cq_ev")
                for c in range(2):
                    V.tensor_copy(ckv[c][:, PAST_A:META2], past[:, c, 0:96])
                    V.tensor_copy(ckv[c][:, META2:PAST_B], ckv[c][:, 0:NMETA])
                    V.tensor_copy(ckv[c][:, PAST_B:KEY_END], past[:, c, 96:PAST])
                    ins = V.memset(ckv[c][:, KEY_END:KW], 0.0)
                ins.then_inc(S["ckv_full"], 1)
                w("kpe_new", 1)
                V.memset(kpe[:, KEY_END:KW], 0.0)
                V.tensor_copy(kpe[:, META2:PAST_B], kpe[:, 0:NMETA]).then_inc(S["kpe_meta"], 1)
                split(18)
                scaled(U_CQ[2], cq[2], rs, "cq_ev")
                split(19)
                scaled(U_CQ[3], cq[3], rs, "cq_ev")
                split(20)
                scaled(U_CQ[4], cq[4], rs, "cq_ev")
                split(21)
                V.tensor_copy(hbuf[:, 3, 1:2], xc[3][:, TOK - 1:TOK]).then_inc(S["hid_out"], 1)
                for c in range(6):
                    w("cq_hi", c + 1)
                    lo(cql[c][:, :], cq[c][:, :], cqh[c][:, :], "cq_lo", col(V_QG + c))
                    if c == 0:
                        scaled(U_CQ[5], cq[5], rs, "cq_ev")
                split(22)
                w("kv_out", 32)
                for c in range(2):
                    w("ckv_hi", c + 1)
                    lo(ckvl[c][:, :], ckv[c][:, :], ckvh[c][:, :], "ckv_lo")
                rstd(rs, 3)
                scaled(U_UQ[0], qn[0], rs, "qn")
                split(23)
                scaled(U_UQ[1], qn[1], rs, "qn")
                split(24)
                scaled(U_UQ[2], qn[2], rs, "qn")
                split(25)
                scaled(U_UQ[3], qn[3], rs, "qn")
                split(26)
                scaled(U_UQ[4], qr[0], rs, "qr_ev")
                wait_alone(dve, "qr_ev", L * PER["qr_ev"] + 1)
                rotate(qr[0][:, :], rtmp[:, :], "qr")
                split(27)
                scaled(U_UQ[5], qr[1], rs, "qr_ev")
                wait_alone(dve, "qr_ev", L * PER["qr_ev"] + 2)
                w("qr", 1)
                rotate(qr[1][:, :], rtmp[:, :], "qr")
                w("y_sum", 3)
                w("mm", U_SY + 1)
                V.memset(vh[:, :].bitcast(F32).rearrange("p (t d) -> p t d", d=65)[:, :, 64:65], 1.0)
                V.memset(vl[:, :].bitcast(F32).rearrange("p (t d) -> p t d", d=65)[:, :, 64:65], 0.0).then_inc(S["v_one"], 1)
                rstd(rs, 4)
                split(28)
                for t in range(10):
                    w("v_hi", t + 1)
                    hi = vh[:, VW * t:VW * (t + 1)].rearrange("p (h d) -> p h d", h=NH)[:, :, 0:64]
                    dst = vl[:, VW * t:VW * (t + 1)].rearrange("p (h d) -> p h d", h=NH)[:, :, 0:64]
                    V.tensor_tensor(dst, ps[:, 3 * ((U_V + t) % 2), :].rearrange("p (h d) -> p h d", h=NH), hi.bitcast(F32), ALU.subtract)\
                        .then_inc(S["v_lo"], 1)
                for c in range(4):
                    V.tensor_tensor(g[c][:, :], g[c][:, :], rs[:, :], ALU.mult).then_inc(S["y_n"], 1)
                split(29)
                split(30)

                w("kpe_out", 16)
                for e in range(2):
                    w("kslot_hi", e + 1)
                    lo(ks[e][1][PE_ROWS[e], :], kpe[PE_ROWS[e], :], ks[e][0][PE_ROWS[e], :], "kslot_lo")

                def load_lo(h):
                    j, e = h // 2, h % 2
                    w("q_hi", h + 1)
                    if h == 0:
                        w("kslot_lo", 2)
                    for dst, src, rows in ((qs[e], qn[j], half(e)), (qs[e], ra[j], PE_ROWS[e]), (ks[e], kf[j], half(e))):
                        ins = V.tensor_tensor(dst[1][rows, :], src[rows, :], dst[0][rows, :].bitcast(F32), ALU.subtract)
                    ins.then_inc(S["q_lo"], 1)

                def reduce_max(h, s):
                    w("mxmm", h * NMX + s + 1)
                    if s == 0 and h:
                        w("mxt", h)
                    for lo_, hi_, c0, n, second, c in MAXES[s][2]:
                        dst = (mx2 if second else mx)[lo_:hi_, c:c + 1]
                        ins = V.reduce_max(dst, ps[lo_:hi_, 3:5, :].rearrange("p a n -> p (a n)")[:, c0:c0 + n], AX_X)
                    ins.then_inc(S["mxred"], 1)

                def both_halves(h):
                    w("mxred", (h + 1) * NMX)
                    V.tensor_tensor(mx[64:P, 0:8], mx[64:P, 0:8], mx2[64:P, :], ALU.max).then_inc(S["mxc"], 1)

                def shift_lo(h):
                    w("mt_hi", h + 1)
                    V.scalar_tensor_tensor(out=mtl[0:10, :], in0=ps[0:10, 3, 0:P], scalar=-1.0, in1=mth[0:10, :].bitcast(F32),
                                           op0=ALU.mult, op1=ALU.subtract).then_inc(S["mt_lo"], 1)

                def sums_out(h):
                    w("pv", (h + 1) * NP)
                    if h >= 2:
                        w("sum_out", 16 * (h - 1))
                    r = slice(64 * (h % 2), 64 * (h % 2) + 1)
                    V.tensor_copy(srow[r, 0:272], ps[64:65, 5, 0:272])
                    V.tensor_copy(srow[r, STREAM:TOK], ps[64:65, 5, 272:272 + DEC])
                    V.tensor_copy(srow[r, 272:STREAM].rearrange("p (a n) -> p a n", a=2), ps[64:65, 6:8, 0:384]).then_inc(S["s_ev"], 1)

                def invert(j):
                    w("sum_in", 16 * (j + 1))
                    V.reciprocal(comp[:, :], comp[:, :]).then_inc(S["inv"], 1)

                def divide(j):
                    w("inv_in", 32 * (j + 1))
                    w("o_ev", 2 * j + 2)
                    V.memset(o[j][:, TOK:T], 0.0)
                    V.tensor_tensor(o[j][:, 0:TOK], o[j][:, 0:TOK], rc[:, 0:TOK], ALU.mult).then_inc(S["o"], 1)

                load_lo(0)
                for s in range(NMX):
                    reduce_max(0, s)
                both_halves(0)
                shift_lo(0)
                for h in range(NH):
                    for i in range(NP):
                        gi = h * NP + i
                        _, _, rows, _, n, diag = PAIRS[i]
                        kind = "d" if diag else "n"
                        before = sum(1 for x_ in PAIRS[:i] if x_[5] == diag) + h * sum(1 for x_ in PAIRS if x_[5] == diag)
                        buf = (pd if diag else pn)[before % 2]
                        w("p", gi + 1)
                        if gi >= 3:
                            w("pv", gi - 2)
                        V.tensor_copy(ph[gi % 3][0:rows, 0:n], buf[0:rows, 0:n]).then_inc(S["p_hi"], 1)
                        if i == 0 and h >= 1:
                            sums_out(h - 1)
                        if h + 1 < NH:
                            if i == 1:
                                load_lo(h + 1)
                            if MX_FROM <= i < MX_FROM + NMX:
                                reduce_max(h + 1, i - MX_FROM)
                            if i == MX_FROM + NMX:
                                both_halves(h + 1)
                            if i == MX_FROM + NMX + 2:
                                shift_lo(h + 1)
                        if h in (2, 4, 6):
                            if i == 10:
                                invert(h // 2 - 1)
                            if i == NP - 1:
                                divide(h // 2 - 1)
                sums_out(NH - 1)

                for c in range(4):
                    w("y_hi", c + 1)
                    lo(yl[c][:, :], g[c][:, :], yh[c][:, :], "y_lo", col(V_LG + c))
                split(31)
                invert(3)

                def add_up(u, m, name):
                    w("mm", u + 1)
                    V.tensor_tensor(x[m].rearrange("p (c n) -> p c n", c=3), x[m].rearrange("p (c n) -> p c n", c=3), slot(u), ALU.add)\
                        .then_inc(S[name], 1)

                for m in range(8):
                    w(f"x_in{m}", 16)
                    add_up(U_OY[m], m, "oy_ev")
                    if m == 1:
                        split(32)
                        divide(3)
                    if m == 3:
                        split(33)
                    if m == 5:
                        rstd(rs, 5)
                        for j in range(4):
                            V.tensor_tensor(o[j][:, :], o[j][:, :], rs[:, :], ALU.mult).then_inc(S["o_n"], 1)
                    if m == 6:
                        for j in range(4):
                            w("o_hi", j + 1)
                            lo(ol[j][:, :], o[j][:, :], oh[j][:, :], "o_lo", col(V_AG + j))
                        split(34)
                split(35)
                for m in range(8):
                    if m and m % 2 == 0:
                        split(35 + m // 2)
                    w("oy_ev", 8)
                    add_up(U_OO + m, m, "res_add")
                    w("xm_hi", m + 1)
                    lo(xml[m][:, :], x[m], xmh[m][:, :], "xm_lo", col(V_MG + m))
                split(B_MLP + 1)
                w("root", 6)
                V.reciprocal(rs[:, :], rs[:, :]).then_inc(S["rstd"], 1)
                wait_alone(dve, "rstd", L * PER["rstd"] + 6)

                def mlp_group(gg, last):
                    for k in range(2 * GT):
                        if not (last and k >= 2 * GT - 2):
                            b = B_MLP + k + 2
                            dve.wait_ge(S["w_hi"], L * NB + gg * (2 * GT) + (b + 1))
                            V.tensor_tensor(wlo[b % 2][:, :], raw[b % 2][:, :], whi[b % 2][:, :].bitcast(F32), ALU.subtract).then_inc(S["w_lo"], 1)
                        u = U_MLP + k
                        dve.wait_ge(S["mm"], L * NU + gg * (2 * GT) + (u + 1))
                        if k < GT:
                            V.scalar_tensor_tensor(out=chunks(msq), in0=slot(u), scalar=0.0, in1=chunks(rs), op0=ALU.max, op1=ALU.mult)\
                                .then_inc(S["relu"], 1)
                            dve.wait_ge(S["f_hi"], L * PER["f_hi"] + gg * GT + (k + 1))
                            V.tensor_tensor(fl[k][:, :], msq[:, :], fh[k][:, :].bitcast(F32), ALU.subtract).then_inc(S["f_lo"], 1)
                            dve.wait_ge(S["f_lo"], L * PER["f_lo"] + gg * GT + (k + 1))
                        else:
                            m = k - GT
                            if k == GT:
                                dve.wait_ge(S["res_add"], L * PER["res_add"] + gg * 8 + 8)
                            xm3 = x[m].rearrange("p (c n) -> p c n", c=3)
                            V.tensor_tensor(xm3, xm3, slot(u), ALU.add).then_inc(S["res_add"], 1)
                            if last:
                                dve.wait_ge(S["xg_hi"], L * 8 + 8 + (m + 1))
                                lo(xgl[m][:, :], x[m], xgh[m][:, :], "xg_lo", col(V_GNEXT + m))

                with dve.Fori(0, GROUPS - 1) as gg:
                    mlp_group(gg, False)
                mlp_group(GROUPS - 1, True)
            assert chain[0] == DVE_CHAIN, chain
            dve.wait_ge(S["root"], DEPTH * 6 + 1)
            dve.wait_ge(S["x_out"], DEPTH * 128 + 128)
            dve.wait_ge(S["sq"], DEPTH * 8 + 8)
            dve.wait_ge(S["xg_lo"], DEPTH * 8 + 8)
            V.reciprocal(rs[:, :], rs[:, :]).then_inc(S["rstd"], 1)
            dve.wait_ge(S["rstd"], DEPTH * 6 + 1)
            for m in range(8):
                V.scalar_tensor_tensor(out=x[m], in0=x[m], scalar=fg[:, m:m + 1], in1=rs[:, :], op0=ALU.mult, op1=ALU.mult)\
                    .then_inc(S["yout"], 1)

        @block.gpsimd
        def _(pool):
            G = nc.gpsimd

            def save_x(m):
                pool.dma_start(x_scr[m], x[m]).then_inc(S["x_out"], 16)

            pool.wait_ge(S["x_load"], 128)
            for m in range(8):
                save_x(m)
            for m in range(1, 8):
                pool.wait_ge(S["sq"], m + 1)
                if m > 1:
                    pool.wait_ge(S["sq_sum"], m - 1)
                G.tensor_tensor(msq[:, :], msq[:, :], rs[:, :], ALU.add).then_inc(S["sq_sum"], 1)
            with pool.Fori(0, DEPTH) as L:
                def w(name, k, alone=False):
                    assert k > 0, name
                    if alone:
                        wait_alone(pool, name, L * PER[name] + k)
                    else:
                        pool.wait_ge(S[name], L * PER[name] + k)

                def sum_squares(acc, tmp, n, sq, out):
                    for m in range(1, n):
                        w(sq, m + 1)
                        if m > 1:
                            w(out, m - 1)
                        G.tensor_tensor(acc, acc, tmp, ALU.add).then_inc(S[out], 1)

                def cube(c):
                    w("g_sq", c + 1, alone=True)
                    G.tensor_scalar(t2[:, :], t2[:, :], 0.044715, 1.0, ALU.mult, ALU.add).then_inc(S["g_poly"], 1)
                    w("g_poly", c + 1)
                    G.tensor_tensor(t2[:, :], t2[:, :], g[c][:, :], ALU.mult).then_inc(S["g_cube"], 1)

                for c in range(3):
                    cube(c)
                cube(3)
                sum_squares(sqa[:, :], sqt[:, :], 2, "ckv_sq", "ckv_sum")
                w("kpe_meta", 1, alone=True)
                for q in range(4):
                    r = slice(32 * q, 32 * q + 32)
                    pool.dma_start(kpe[r, PAST_A:META2], past_kpe[L, :, 0:96]).then_inc(S["kpe"], 16)
                    pool.dma_start(kpe[r, PAST_B:KEY_END], past_kpe[L, :, 96:PAST]).then_inc(S["kpe"], 16)
                pool.dma_start(kpe_out[L], kpe[0:ROPE, 0:TOK]).then_inc(S["kpe_out"], 16)
                w("ckv_full", 1, alone=True)
                for c in range(2):
                    pool.dma_start(ckv_out[L, c], ckv[c][:, 0:TOK]).then_inc(S["kv_out"], 16)
                sum_squares(sqa[:, :], sqt[:, :], 6, "cq_sq", "cq_sum")
                w("hid_out", 1, alone=True)
                pool.dma_start(h_out[L], hbuf[:, :, :]).then_inc(S["small_out"], 16)
                pool.dma_start(conv_out[L], cbuf[:, :, :, :]).then_inc(S["small_out"], 16)
                sum_squares(t3[:, :], t4[:, 0:T], 4, "y_sq", "y_sum")

                w("kf", 4)
                w("qr", 2)
                w("ra", 16 * NH, alone=True)
                n_row = 0
                for k in range(2):
                    for dst, value in ((pd[k][:, 0:64], 0.0), (ks[0][k][96:97, :].bitcast(F32), 1.0 - k), (ks[1][k][32:64, :].bitcast(F32), 0.0),
                                       (qs[0][k][96:97, :].bitcast(F32), 0.0), (qs[1][k][32:64, :].bitcast(F32), 0.0)):
                        G.memset(dst, value).then_inc(S["row_set"], 1)
                        n_row += 1
                        w("row_set", n_row, alone=True)
                G.memset(ks[1][0][32:33, :].bitcast(F32), 1.0).then_inc(S["slot_const"], 1)
                for h in range(NH):
                    for i in range(NP):
                        gi = h * NP + i
                        _, _, rows, _, n, diag = PAIRS[i]
                        before = sum(1 for x_ in PAIRS[:i] if x_[5] == diag) + h * sum(1 for x_ in PAIRS if x_[5] == diag)
                        buf = (pd if diag else pn)[before % 2]
                        if i == 0 and h % 2 == 0 and h:
                            w("s", h * NP, alone=True)
                            w("p_lo", h * NP)
                            G.memset(qs[1][0][32:33, :].bitcast(F32), 0.0).then_inc(S["q_zero"], 1)
                            w("q_zero", h // 2)
                        elif gi == 0:
                            w("slot_const", 1)
                        w("p_hi", gi + 1)
                        G.tensor_tensor(pl[gi % 3][0:rows, 0:n], buf[0:rows, 0:n], ph[gi % 3][0:rows, 0:n].bitcast(F32), ALU.subtract)\
                            .then_inc(S["p_lo"], 1)
                sum_squares(osq[:, :], osqt[:, :], 4, "o_sq", "o_sum")
                sum_squares(msq[:, :], rs[:, :], 8, "xm_sq", "xm_sum")
                for m in range(8):
                    w("res_add", GROUPS * 8 + m + 1, alone=True)
                    save_x(m)
                    if m:
                        pool.wait_ge(S["sq"], L * 8 + 8 + m + 1)
                        if m > 1:
                            pool.wait_ge(S["sq_sum"], L * 7 + 7 + m - 1)
                        G.tensor_tensor(msq[:, :], msq[:, :], rs[:, :], ALU.add).then_inc(S["sq_sum"], 1)
            pool.wait_ge(S["x_out"], DEPTH * 128 + 128)
            pool.wait_ge(S["kpe_out"], DEPTH * 16)
            pool.wait_ge(S["kv_out"], DEPTH * 32)
            pool.wait_ge(S["small_out"], DEPTH * 32)


_OUTS = [("yT", (8, P, T)), ("ckv_out", (DEPTH, 2, P, TOK)), ("kpe_out", (DEPTH, ROPE, TOK)), ("h_out", (DEPTH, P, 4, 2)),
         ("conv_out", (DEPTH, P, 4, 2, CW - 1))]


def kernel(**inputs):
    import concourse.bacc as _bacc
    from concourse.bass_utils import run_bass_kernel_spmd as _run

    a = {k: np.asarray(v) for k, v in inputs.items()}
    f32 = np.float32

    tokens = np.concatenate([a["meta_tokens"], a["x_prompt"][0], a["x_sample"][0], np.zeros((2, DM), f32)], 0)
    arrays = {"xT": np.ascontiguousarray(tokens.T).reshape(8, P, T)}

    def block(w):
        k, m = w.shape
        return w.reshape(k // P, P, m).transpose(1, 0, 2).reshape(P, -1)

    wst = np.zeros((DEPTH * NB, P, 1024), f32)
    s0, s1, s2, s3 = QL, QL + KVL, QL + KVL + ROPE, QL + KVL + ROPE + LRU
    for l in range(DEPTH):
        def put(b, w):
            wst[l * NB + b, :, 0:w.shape[1]] = w

        w_in = a["w_in"][l]
        for c in range(4):
            put(B_XR[c], block(w_in[:, s2 + P * c:s2 + P * c + P]))
            put(B_GR[c], block(w_in[:, s3 + P * c:s3 + P * c + P]))
            gate = np.zeros((P, 2 * P), f32)
            for n, name in enumerate(("w_gate_a", "w_gate_x")):
                for i in range(2):
                    gate[64 * i:64 * i + 64, P * n + 64 * i:P * n + 64 * i + 64] = a[name][l, 2 * c + i]
            put(B_GATE[c], gate)
        for c in range(2):
            put(B_CKV[c], block(w_in[:, s0 + P * c:s0 + P * c + P]))
        put(B_KR, block(np.concatenate([w_in[:, s1:s2]] * 4, 1)))
        for c in range(6):
            put(B_CQ[c], block(w_in[:, P * c:P * c + P]))
        uq = a["w_uq"][l].reshape(QL, NH, NOPE + ROPE)
        nope, rot = uq[:, :, 0:NOPE].reshape(QL, -1), uq[:, :, NOPE:].reshape(QL, -1)
        for c in range(4):
            put(B_UQ + c, block(nope[:, P * c:P * c + P]))
        for c in range(2):
            put(B_UQ + 4 + c, block(rot[:, P * c:P * c + P]))
        ukv = a["w_ukv"][l].reshape(KVL, NH, NOPE + VD)
        put(B_UV, block(ukv[:, :, NOPE:].reshape(KVL, -1)))
        uk = ukv[:, :, 0:NOPE].reshape(KVL, -1)
        put(B_UK, np.concatenate([block(uk[:, P * j:P * j + P]) for j in range(4)], 1))
        wo = a["w_out"][l]
        for i, ms in enumerate(OY_TILES):
            put(B_OY + i, np.concatenate([block(wo[ATT:, P * m:P * m + P]) for m in ms], 1))
        for i in range(4):
            put(B_OO + i, np.concatenate([block(wo[0:ATT, P * m:P * m + P]) for m in (2 * i, 2 * i + 1)], 1))
        up, down = a["w_up"][l], a["w_down"][l]
        for q in range(GROUPS):
            for k in range(GT):
                f = GT * q + k
                put(B_MLP + 2 * GT * q + k, block(up[:, P * f:P * f + P]))
                put(B_MLP + 2 * GT * q + GT + k, block(down[1024 * q:1024 * q + 1024, P * k:P * k + P]))
    arrays["wst"] = wst

    def cols(v):
        return v.reshape(-1, P).T

    vec = np.zeros((DEPTH, P, NVEC), f32)
    for l in range(DEPTH):
        cw = a["conv_w"][l].reshape(CW, 4, P).transpose(2, 1, 0).reshape(P, 16)
        parts = [cols(a["norm_mix_g"][l]), cols(a["q_norm_g"][l]), cols(a["kv_norm_g"][l]), cw, cols(a["conv_b"][l]), cols(a["b_gate_a"][l]),
                 cols(a["b_gate_x"][l]), cols(a["lru_lambda"][l]), cols(a["attn_out_g"][l]), cols(a["lru_out_g"][l]), cols(a["norm_mlp_g"][l]),
                 cols(a["norm_mix_g"][min(l + 1, DEPTH - 1)])]
        vec[l] = np.concatenate(parts, 1)
    arrays["vec"] = vec
    arrays["fgain"] = np.ascontiguousarray(cols(a["final_norm_g"]))

    pos = np.concatenate([np.arange(-NMETA, SEQ), PAST + np.arange(DEC), np.zeros(2)]).astype(f32)
    inv = (f32(10000.0) ** (-np.arange(0, ROPE, 2, dtype=f32) / f32(ROPE))).astype(f32)
    ang = inv[:, None] * pos[None, :]
    cos, sin = np.cos(ang).astype(f32), np.sin(ang).astype(f32)
    arrays["ropeC"] = np.tile(np.concatenate([cos, cos], 0), (4, 1))
    arrays["ropeS"] = np.tile(np.concatenate([-sin, sin], 0), (4, 1))
    arrays["consts"] = np.stack([np.eye(P, dtype=f32), np.ones((P, P), f32)])
    arrays["past_ckv"] = np.ascontiguousarray(a["cache_ckv"][:, 0].transpose(0, 2, 1).reshape(DEPTH, 2, P, PAST).transpose(0, 2, 1, 3))
    arrays["past_kpe"] = np.ascontiguousarray(a["cache_kpe"][:, 0].transpose(0, 2, 1))
    arrays["h0"] = np.ascontiguousarray(a["state_lru_h"][:, 0].reshape(DEPTH, 4, P).transpose(0, 2, 1))
    arrays["conv0"] = np.ascontiguousarray(a["state_conv"][:, 0].reshape(DEPTH, CW - 1, 4, P).transpose(0, 3, 2, 1))

    nc = _bacc.Bacc("TRN2", target_bir_lowering=False, num_devices=1)
    args = [nc.dram_tensor(f"in_{n}", v.shape, F32, kind="ExternalInput").ap() for n, v in arrays.items()]
    args += [nc.dram_tensor(f"out_{n}", s, F32, kind="ExternalOutput").ap() for n, s in _OUTS]
    args += [nc.dram_tensor("x_scratch", (8, P, T), F32, kind="Internal").ap(), nc.dram_tensor("sum_scratch", (NH, TOK), F32, kind="Internal").ap()]
    trunk(nc, *args)
    res = _run(nc, [{f"in_{n}": v for n, v in arrays.items()}], core_ids=[0]).results[0]
    yT, ckv, kpe, hs, cv = (res[f"out_{n}"] for n, _ in _OUTS)

    y = yT.reshape(DM, T).T
    ckv = ckv.reshape(DEPTH, KVL, TOK).transpose(0, 2, 1)
    kpe = kpe.transpose(0, 2, 1)
    hs = hs.transpose(3, 0, 2, 1).reshape(2, DEPTH, 1, LRU)
    cv = cv.transpose(3, 0, 4, 2, 1).reshape(2, DEPTH, 1, CW - 1, LRU)
    p, s = slice(NMETA, STREAM), slice(STREAM, TOK)
    out = (y[None, p], y[None, s], ckv[:, None, p], kpe[:, None, p], hs[0], cv[0], ckv[:, None, s], kpe[:, None, s], hs[1], cv[1])
    return tuple(np.ascontiguousarray(v) for v in out)
```

```python
from contextlib import ExitStack

import numpy as np
import concourse.bass as bass
from concourse import mybir

F32 = mybir.dt.float32
F32R = mybir.dt.float32r
ALU = mybir.AluOpType
ACT = mybir.ActivationFunctionType
AX_X = mybir.AxisListType.X

P = 128
DM, SEQ, DEPTH, DEC, PAST = 1024, 1024, 2, 32, 128
NMETA, QL, KVL, ROPE, NOPE, NH, LRU, ATT, CW, DFF = 16, 768, 256, 32, 64, 8, 512, 512, 4, 4096
VD = 64
EPS = 1e-6
SM_SCALE = float((NOPE + ROPE) ** -0.5)
STREAM = NMETA + SEQ
TOK = STREAM + DEC
T = TOK + 2
CH = T // 3
KW = 1296
KCH = KW // 3
PAST_A, META2, PAST_B, KEY_END = TOK, TOK + 96, TOK + 96 + NMETA, TOK + 96 + NMETA + 32
GELU_C = float(np.sqrt(2.0 / np.pi))

B_XR, B_GR, B_CKV, B_KR = [0, 1, 2, 3], [5, 6, 8, 9], [11, 12], 14
B_GATE = [4, 7, 10, 13]
B_CQ = [15, 16, 17, 18, 19, 20]
B_UQ, B_UV, B_UK = 21, 27, 28
B_OY, B_OO, B_MLP = 29, 34, 38
GROUPS, GT = 4, 8
NB = B_MLP + GROUPS * 2 * GT

U_SMIX = 0
U_XR, U_GATE, U_GR, U_CKV = [1, 2, 3, 4], [5, 9, 13, 17], [7, 8, 11, 12], [15, 16]
U_KR, U_SKV, U_SQ = 19, 21, 28
U_CQ = [20, 22, 23, 24, 25, 26]
U_UQ = [27, 29, 30, 31, 32, 33]
U_SY, U_V, U_K = 34, 35, 45
U_OY, U_SO, U_OO, U_SMLP, U_MLP = [49, 50, 51, 53, 54, 55, 56, 57], 52, 58, 66, 67
NU = U_MLP + GROUPS * 2 * GT

READ = {U_SMIX: ("root", 1), U_KR: ("kr_ev", 1), U_SKV: ("root", 2), U_SQ: ("root", 3), U_SY: ("root", 4), U_SO: ("root", 5), U_SMLP: ("root", 6)}
for _c in range(4):
    READ[U_XR[_c]] = ("xr_ev", _c + 1)
    READ[U_GR[_c]] = ("gr_ev", _c + 1)
    READ[U_GATE[_c]] = ("gate_r", _c + 1)
    READ[U_GATE[_c] + 1] = ("gate_i", _c + 1)
    READ[U_UQ[_c]] = ("qn_raw", _c + 1) if _c < 2 else ("qn", _c + 1)
    READ[U_K + _c] = ("kf", _c + 1)
for _c in range(2):
    READ[U_CKV[_c]] = ("ckv_ev", _c + 1)
    READ[U_UQ[4 + _c]] = ("qr_ev", _c + 1)
for _c in range(6):
    READ[U_CQ[_c]] = ("cq_ev", _c + 1)
for _c in range(8):
    READ[U_OY[_c]] = ("oy_ev", _c + 1)
    READ[U_OO + _c] = ("res_add", _c + 1)
for _c in range(10):
    READ[U_V + _c] = ("v_lo", _c + 1)

LAST_UNIT = {}
for _c in range(4):
    LAST_UNIT[B_XR[_c]] = U_XR[_c]
    LAST_UNIT[B_GR[_c]] = U_GR[_c]
    LAST_UNIT[B_GATE[_c]] = U_GATE[_c] + 1
    LAST_UNIT[B_OO + _c] = U_OO + 2 * _c + 1
for _c in range(2):
    LAST_UNIT[B_CKV[_c]] = U_CKV[_c]
for _c in range(6):
    LAST_UNIT[B_CQ[_c]] = U_CQ[_c]
    LAST_UNIT[B_UQ + _c] = U_UQ[_c]
LAST_UNIT[B_KR], LAST_UNIT[B_UV], LAST_UNIT[B_UK] = U_KR, U_V + 9, U_K + 3
OY_ORDER = [5, 6, 7, 0, 1, 2, 3, 4]
OY_TILES = [OY_ORDER[0:2], OY_ORDER[2:4], OY_ORDER[4:6], OY_ORDER[6:7], OY_ORDER[7:]]
for _c, _m in enumerate(OY_TILES):
    LAST_UNIT[B_OY + _c] = U_OY[OY_ORDER.index(_m[-1])]
for _c in range(2 * GT * GROUPS):
    LAST_UNIT[B_MLP + _c] = U_MLP + _c

WCOLS = {b: 1024 for b in range(NB)}
for _c in range(4):
    WCOLS[B_GATE[_c]] = 256
for _c in range(6):
    WCOLS[B_UQ + _c] = 768
WCOLS[B_OY + 3] = WCOLS[B_OY + 4] = 512

V_GMIX, V_QG, V_KVG, V_CW, V_CB, V_BA, V_BX, V_LAM, V_AG, V_LG, V_MG, V_GNEXT = 0, 8, 14, 16, 32, 36, 40, 44, 48, 52, 56, 64
NVEC = 72

META_ROWS = NMETA
PAIRS = [(9, META2, META_ROWS, 0, 272, 0), (9, META2, META_ROWS, 272, 384, 0), (9, META2, META_ROWS, 656, 384, 0)]
for _t in range(8):
    _q = NMETA + 128 * _t
    for _lo, _hi in ((0, 272), (272, 656), (656, STREAM)):
        if _hi > _q:
            _q0 = max(_q, _lo)
            PAIRS.append((_t, NMETA + 128 * _t, P, _q0, _hi - _q0, 1 if _q0 == _q else 0))
SAMPLE_PAIRS = [(8, STREAM, P, STREAM, DEC, 0), (9, META2, NMETA + 32, STREAM, DEC, 0)]
_DIAG = sorted((x for x in PAIRS if x[5]), key=lambda x: {0: 0, 2: 1, 5: 2}.get(x[0], 3 + x[0]))
_REST = [x for x in PAIRS if not x[5]]
_REST = _REST[:-1] + SAMPLE_PAIRS[:1] + _REST[-1:] + SAMPLE_PAIRS[1:]
PAIRS = [y for x in zip(_REST, _DIAG) for y in x] + _REST[len(_DIAG):]
NP = len(PAIRS)
LAG = 3
MX_AT = [3, 4, 5, 6, 7, 8, 9, 10]
MX_END = MX_AT[-1] + 1
DVE_CHAIN = 82
VTILES = [NMETA + 128 * t for t in range(8)] + [STREAM, META2]
VW = 65 * NH


def o_place(q0):
    if q0 >= STREAM:
        return 5, 272 + q0 - STREAM
    if q0 < 272:
        return 5, q0
    return (6, q0 - 272) if q0 < 656 else (7, q0 - 656)


def group(q0):
    return 3 if q0 >= STREAM else 0 if q0 < 272 else 1 if q0 < 656 else 2


FIRST = [min(i for i, x in enumerate(PAIRS) if group(x[3]) == g) for g in range(4)]
LAST = [max(i for i, x in enumerate(PAIRS) if group(x[3]) == g) for g in range(4)]

MAXES = []
for _t in range(7):
    _q, _n = NMETA + 128 * _t, NMETA + 128 * (_t + 1)
    _b = [(0, _q, 0, max(256, min(_n, 512)))]
    if _n > 512:
        _b.append((1, _q, 512 if _n - 512 > 64 else _n - 256, max(256, _n - 512)))
    if _t == 3:
        _r = [(0, P, 0, _n - 64, 0, 3), (64, P, 512 + 192, 64, 1, 3)]
    else:
        _r = [(0, P, 0, _n - 64, 0, _t), (64, P, _n - 64, 64, 1, _t)]
    MAXES.append((_b, _r))
MAXES.append(([(0, NMETA + 896, 0, 512), (1, NMETA + 896, 512, 464)], [(0, P, 0, 976, 0, 7)]))
MAXES.append(([(0, NMETA + 896, 784, 256)], [(64, P, 192, 64, 1, 7)]))
MAXES.append(([(0, 0, 0, 256)], [(0, NMETA, 0, NMETA, 0, 8)]))
MAXES.append(([(0, TOK - P, STREAM, 256)], [(96, P, 0, KEY_END - STREAM, 0, 9)]))


def _both(a, b):
    return a[0] + [(1, *x[1:]) for x in b[0]], a[1] + [(lo, hi, 512 + c0, *rest) for lo, hi, c0, *rest in b[1]]


MAXES = [_both(MAXES[0], MAXES[1]), _both(MAXES[2], MAXES[9]), *MAXES[3:8], _both(MAXES[8], MAXES[10])]
NMX = len(MAXES)


BUF, P32_BEFORE, PH_BEFORE = [], [], []
for _g in range(NH * NP):
    _same = [g for g in range(_g) if PAIRS[g % NP][5] == PAIRS[_g % NP][5]]
    _ring = 2 if PAIRS[_g % NP][5] else 3
    BUF.append((len(_same) % 2, len(_same) % _ring))
    P32_BEFORE.append(_same[-2] if len(_same) >= 2 else None)
    PH_BEFORE.append(_same[-_ring] if len(_same) >= _ring else None)


def trunk(nc, xT, wst, vec, fgain, ropeC, ropeS, ident_in, past_ckv, past_kpe, h0, conv0,
          yT, ckv_out, kpe_out, h_out, conv_out, x_scr, sum_scr):
    ctx = ExitStack()
    with ctx:
        enter = ctx.enter_context

        TB, KB = T * 4, KW * 4
        total = 6 * 4096 + 8 * TB + 16 * TB + 8 * TB + 64 + 4 * TB + 2 * KB + KB + 2 * TB + TB
        base = -(-nc.sbuf_base // 32) * 32
        enter(nc.sbuf_tensor("arena", [P, (total + 64) // 4], F32))
        regions = {}
        at = base
        for name, size in (("W", 6 * 4096), ("X", 8 * TB), ("R", 16 * TB), ("F", 8 * TB + 64), ("G", 4 * TB),
                           ("CK", 2 * KB), ("KP", KB), ("CS", 2 * TB), ("RS", TB)):
            regions[name] = at
            at += size

        def place(name, region, offset, cols, dt=F32):
            return nc.alloc_sbuf_tensor_at(name, [P, cols], dt, offset=regions[region] + offset, align_bytes=8)

        def tiles(name, region, first, n, dt=F32):
            return [place(f"{name}{i}", region, (first + i) * TB, T, dt) for i in range(n)]

        raw = [place(f"raw{i}", "W", i * 4096, 1024) for i in range(2)]
        whi = [place(f"whi{i}", "W", (2 + i) * 4096, 1024, F32R) for i in range(2)]
        wlo = [place(f"wlo{i}", "W", (4 + i) * 4096, 1024, F32R) for i in range(2)]
        xall = place("xall", "F", 0, 8 * T)
        x = [xall[:, m * T:(m + 1) * T] for m in range(8)]
        xgh, xgl = tiles("xgh", "R", 8, 8, F32R), tiles("xgl", "R", 0, 8, F32R)
        xc = tiles("xc", "F", 0, 4)
        t1, t2, t3 = tiles("t", "F", 4, 3)
        t4 = place("t4", "F", 7 * TB, T + 16)
        g = tiles("g", "G", 0, 4)
        ckv = [place(f"ckv{i}", "CK", i * KB, KW) for i in range(2)]
        kpe = place("kpe", "KP", 0, KW)
        cosT, sinT = tiles("rope", "CS", 0, 2)
        cq = tiles("cq", "X", 0, 6)
        xch, xcl = tiles("xcs", "X", 6, 2, F32R)
        sqa, sqt = tiles("sqa", "X", 6, 2)
        rs = place("rs", "RS", 0, T)
        cqh, cql = tiles("cqh", "R", 0, 6, F32R), tiles("cql", "R", 8, 6, F32R)
        ckvh = [place("ckvh0", "R", 6 * TB, KW, F32R), place("ckvh1", "R", 14 * TB, KW, F32R)]
        ckvl = [place(f"ckvl{i}", "CK", i * KB, KW, F32R) for i in range(2)]
        qn, qr = tiles("qn", "X", 0, 4), tiles("qr", "X", 4, 2)
        rtmp = place("rtmp", "X", 6 * TB, T)
        kf = [place(f"kf{i}", "R", 8 * TB + i * KB, KW) for i in range(4)]
        ra = [place(f"ra{i}", "F", 20992 + i * TB, T) for i in range(3)] + [place("ra3", "R", 20992, T)]
        vh, vl = place("vh", "F", 0, 10 * VW, F32R), place("vl", "R", 0, 10 * VW, F32R)
        qs = [[place("qeh", "R", 6 * TB, T, F32R), place("qel", "R", 7 * TB, T, F32R)],
              [place("qoh", "CS", 0, T, F32R), place("qol", "CS", TB, T, F32R)]]
        ke = 8 * TB + 4 * KB
        ks = [[place("keh", "R", ke, KW, F32R), place("kel", "R", ke + KB, KW, F32R)],
              [place("koh", "CK", 0, KW, F32R), place("kol", "CK", KB, KW, F32R)]]
        pd = [place(f"pd{i}", "X", 4 * TB + 1536 * i, 384) for i in range(2)]
        pn = [place(f"pn{i}", "X", 4 * TB + 1536 * (2 + i), 384) for i in range(2)]
        phd = [place(f"phd{i}", "X", 4 * TB + 1536 * (4 + i), 384, F32R) for i in range(2)]
        phn = [place(f"phn{i}", "RS", 1536 * i, 384, F32R) for i in range(2)] + [place("phn2", "R", ke + 2 * KB, 384, F32R)]
        pl = [place(f"pl{i}", "X", 4 * TB + 1536 * (6 + i), 384, F32R) for i in range(2)]
        pl.append(place("pl2", "R", ke + 2 * KB + 1536, 384, F32R))

        def p_buffers(g):
            n32, nh = BUF[g]
            return ((pd[n32], phd[nh]) if PAIRS[g % NP][5] else (pn[n32], phn[nh])) + (pl[g % 3],)

        rc = place("rc", "X", 4 * TB + 1536 * 8, T)
        srow = place("srow", "KP", 0, T)
        o = tiles("o", "X", 0, 4)
        yh = tiles("yh", "R", 8, 4, F32R)
        yl = tiles("yl", "R", 12, 4, F32R)
        oh, ol = tiles("oh", "X", 4, 4, F32R), tiles("ol", "X", 0, 4, F32R)
        osq = place("osq", "CK", 0, T)
        osqt = place("osqt", "CK", TB, T)
        msq = place("msq", "CS", TB, T)
        xmh, xml = tiles("xmh", "R", 8, 8, F32R), tiles("xml", "R", 0, 8, F32R)
        fh, fl = tiles("fh", "X", 0, 8, F32R), tiles("fl", "G", 0, 8, F32R)

        def sb(name, shape, dt=F32):
            return enter(nc.sbuf_tensor(name, shape, dt))

        vecs = sb("vecs", [P, NVEC])
        fg = sb("fg", [P, 8])
        half_ba, half_bx = sb("half_ba", [P, 4]), sb("half_bx", [P, 4])
        sp2, spw = sb("sp2", [P, 4]), sb("spw", [P, 16])
        eps = sb("eps", [P, 1])
        ones = sb("ones", [P, P])
        ident = sb("ident", [P, P])
        past = sb("past", [P, 2, PAST])
        xs = sb("xs", [P, 4, CW - 1 + DEC + 2])
        cbuf = sb("cbuf", [P, 4, 2, CW - 1])
        hbuf = sb("hbuf", [P, 4, 2])
        h0s = sb("h0s", [P, 4])
        mx, mx2 = sb("mx", [P, P]), sb("mx2", [P, 8])
        mth, mtl = sb("mth", [16, P], F32R), sb("mtl", [16, P], F32R)
        comp = nc.alloc_sbuf_tensor_at("comp", [16, 2 * TOK // 16], F32, offset=regions["KP"] + TB, align_bytes=8)
        ps = enter(nc.psum_tensor("ps", [P, 8, 512], F32))

        PER = {}

        def sem(name, per_layer=0):
            s = enter(nc.semaphore(name))
            PER[name] = per_layer
            S[name] = s

        S = {}
        for name, per in (
            ("dve_chain", DVE_CHAIN), ("raw0", 16 * NB // 2), ("raw1", 16 * NB // 2), ("w_hi", NB), ("w_lo", NB), ("mm", NU),
            ("vec_in", 64), ("table_in", 32), ("const_in", 0), ("const_set", 0),
            *((f"x_in{m}", 16) for m in range(8)), *((f"x_load{m}", 0) for m in range(8)), ("x_out", 16 * 8), ("xg_hi", 8), ("xg_lo", 8), ("sq", 8), ("sq_sum", 7),
            ("root", 6), ("rstd", 6),
            ("xr_ev", 4), ("conv", 4), ("xc_hi", 4), ("xc_lo", 4),
            ("gate_r", 4), ("gate_t", 4), ("gate_i", 4), ("root_t", 4), ("lru_w", 4), ("hid", 4),
            ("gr_ev", 4), ("g_sq", 4), ("g_cube", 4), ("g_tanh", 4), ("y", 4),
            ("ckv_ev", 2), ("ckv_sq", 2), ("ckv_sum", 1), ("ckv_n", 2), ("ckv_hi", 2), ("ckv_lo", 2),
            ("kr_ev", 1), ("kpe_new", 1), ("kpe_meta", 1), ("kpe", 16 * 8), ("kpe_out", 16), ("kv_out", 32), ("ckv_full", 1), ("hid_out", 1), ("small_out", 32), ("g_poly", 4), ("spw_abs", 1), ("spw_exp", 1), ("sp2", 1),
            ("cq_ev", 6), ("cq_sq", 6), ("cq_sum", 5), ("cq_hi", 6), ("cq_lo", 6),
            ("qn_raw", 2), ("qn", 4), ("qr_ev", 2), ("qr", 2), ("ra0", 16 * 4), ("ra1", 16 * 4),
            ("y_sq", 4), ("y_sum", 3), ("y_n", 4), ("v_one", 1), ("v_hi", 10), ("v_lo", 10), ("kf", 4),
            ("kslot_hi", 2), ("kslot_lo", 2),
            ("slot_const", 1), ("row_set", 12), ("q_hi", NH), ("q_lo", NH), ("s", NH * NP), ("p", NH * NP), ("p_lo", NH * NP),
            ("pv", NH * NP), ("mxmm", NH * NMX), ("mxred", NH * NMX), ("mxc", NH), ("mxt", NH), ("mt_hi", NH), ("mt_lo", NH),
            ("aug", 16 * 6 * NH), ("o_ev", 2 * NH), ("s_ev", 2 * NH), ("sum_out", 16 * NH), ("sum_in", 16 * 4), ("inv", 4), ("inv_out", 16 * 4),
            ("inv_in", 16 * NH), ("o", 4), ("o_sq", 4), ("o_sum", 3), ("o_n", 4), ("o_hi", 4), ("o_lo", 4),
            ("y_hi", 4), ("y_lo", 4), ("oy_ev", 8), ("xm_hi", 8), ("xm_lo", 8), ("xm_sq", 8), ("xm_sum", 7),
            ("relu", GROUPS * GT), ("f_sq", GROUPS * GT), ("f_hi", GROUPS * GT), ("f_lo", GROUPS * GT), ("res_add", 8 + GROUPS * 8),
            ("yout", 8), ("y_st", 0),
        ):
            sem(name, per)

        block = enter(nc.Block())

        def col(c):
            return vecs[:, c:c + 1]

        def chunks(tile):
            return tile[:, 0:T].rearrange("p (c n) -> p c n", c=3)

        def slot(u):
            return ps[:, 3 * (u % 2):3 * (u % 2) + 3, 0:CH]

        def half(e):
            return slice(64 * e, 64 * e + 64)

        def wait_alone(engine, name, value):
            value = engine.to_reg(value)
            engine.wait_ge(S["const_in"], 64)
            engine.wait_ge(S[name], value)

        PE_ROWS = [slice(64, 96), slice(0, 32)]
        SHIFT_ROW = [96, 32]
        MAX_ROWS, ALL_ROWS = [96, P], [97, P]

        @block.sync
        def _(sp):
            sp.dma_start(ones[:, :], ident_in[1]).then_inc(S["const_in"], 16)
            sp.dma_start(ident[:, :], ident_in[0]).then_inc(S["const_in"], 16)
            sp.dma_start(fg[:, :], fgain).then_inc(S["const_in"], 16)
            for m in range(8):
                sp.dma_start(x[m], xT[m]).then_inc(S[f"x_load{m}"], 16)
            with sp.Fori(0, DEPTH) as L:
                def w(name, k):
                    assert k > 0, name
                    sp.wait_ge(S[name], L * PER[name] + k)

                for n in (0, 1):
                    sp.wait_ge(S["w_lo"], L * NB + 1)
                    sp.dma_start(raw[n][:, :], wst[L * NB + n]).then_inc(S[f"raw{n}"], 16)
                sp.wait_ge(S["xg_hi"], L * 8 + 8)
                sp.wait_ge(S["xg_lo"], L * 8 + 8)
                sp.dma_start(vecs[:, :], vec[L]).then_inc(S["vec_in"], 16)
                sp.dma_start(h0s[:, :], h0[L]).then_inc(S["vec_in"], 16)
                sp.dma_start(xs[:, :, 0:CW - 1], conv0[L]).then_inc(S["vec_in"], 16)
                sp.dma_start(past[:, :, :], past_ckv[L]).then_inc(S["vec_in"], 16)
                w("mm", U_SMIX + 1)
                sp.dma_start(cosT[:, :], ropeC).then_inc(S["table_in"], 16)
                sp.dma_start(sinT[:, :], ropeS).then_inc(S["table_in"], 16)
                with sp.Fori(1, 15) as i:
                    for n in (0, 1):
                        sp.wait_ge(S["w_lo"], L * NB + 2 * i + n)
                        sp.dma_start(raw[n][:, :], wst[L * NB + 2 * i + n]).then_inc(S[f"raw{n}"], 16)

                y_squares_read = sp.to_reg(L * NU + U_SY + 1)
                queries_turned = [sp.to_reg(L * PER["qr"] + 1 + j) for j in range(2)]
                for h in range(NH):
                    if h in (0, 4):
                        sp.wait_ge(S["qr"], queries_turned[h // 4])
                    if h == 0:
                        sp.wait_ge(S["mm"], y_squares_read)
                    src = qr[h // 4][32 * (h % 4):32 * (h % 4) + 32, :]
                    sp.dma_start(ra[h // 2][PE_ROWS[h % 2], :], src).then_inc(S[f"ra{h // 4}"], 16)

                wait_alone(sp, "w_lo", L * NB + 30)
                sp.dma_start(raw[0][:, :], wst[L * NB + 30]).then_inc(S["raw0"], 16)

                for h in range(NH + 1):
                    if h < NH:
                        e = h % 2
                        r = slice(SHIFT_ROW[e], SHIFT_ROW[e] + 1)
                        if h == 0:
                            rows_set = sp.to_reg(L * PER["slot_const"] + 1)
                        w("mt_lo", h + 1)
                        if h == 0:
                            sp.wait_ge(S["slot_const"], rows_set)
                        for part, rows in ((0, mth), (1, mtl)):
                            q, m = qs[e][part][:, :].bitcast(F32), rows[:, :].bitcast(F32)
                            sp.dma_start(q[r, NMETA:STREAM].rearrange("a (t n) -> a t n", t=8), m[0:8, :]).then_inc(S["aug"], 16)
                            sp.dma_start(q[r, 0:NMETA], m[8:9, 0:NMETA]).then_inc(S["aug"], 16)
                            sp.dma_start(q[r, STREAM:TOK], m[9:10, P - DEC:P]).then_inc(S["aug"], 16)
                    if h == 6:
                        w("q_lo", 6)
                        for m in (5, 6, 7):
                            sp.dma_start(x[m], x_scr[m]).then_inc(S[f"x_in{m}"], 16)
                    if h == 0:
                        wait_alone(sp, "w_lo", L * NB + 31)
                        sp.dma_start(raw[1][:, :], wst[L * NB + 31]).then_inc(S["raw1"], 16)
                    if h >= 1:
                        k = h - 1
                        w("s_ev", 2 * (k + 1))
                        sp.dma_start(sum_scr[k:k + 1, :], srow[64 * (k % 2):64 * (k % 2) + 1, 0:TOK]).then_inc(S["sum_out"], 16)
                        if k % 2 == 1:
                            j = k // 2
                            w("sum_out", 16 * (k + 1))
                            flat = sum_scr[2 * j:2 * j + 2, :].rearrange("a (r n) -> (a r) n", r=8)
                            sp.dma_start(comp[:, :], flat).then_inc(S["sum_in"], 16)
                            w("inv", j + 1)
                            sp.dma_start(flat, comp[:, :]).then_inc(S["inv_out"], 16)
                            w("inv_out", 16 * (j + 1))
                            for e in range(2):
                                sp.dma_start(rc[half(e), 0:TOK], sum_scr[2 * j + e:2 * j + e + 1, :].to_broadcast([64, TOK]))\
                                    .then_inc(S["inv_in"], 16)

                with sp.Fori(16, NB // 2) as i:
                    for n in (0, 1):
                        sp.wait_ge(S["w_lo"], L * NB + 2 * i + n)
                        sp.dma_start(raw[n][:, :], wst[L * NB + 2 * i + n]).then_inc(S[f"raw{n}"], 16)
            for m in range(8):
                sp.wait_ge(S["yout"], m + 1)
                sp.dma_start(yT[m], x[m]).then_inc(S["y_st"], 16)
            sp.wait_ge(S["y_st"], 16 * 8)

        @block.tensor
        def _(pe):
            PASSES = (("h", "h"), ("h", "l"), ("l", "h"))

            with pe.Fori(0, DEPTH) as L:
                def w(name, k):
                    assert k > 0, name
                    pe.wait_ge(S[name], L * PER[name] + k)

                def take(u):
                    if u >= 2:
                        w(*READ[u - 2])

                def product(dst, u, b, woff, rhs_h, rhs_l, ready=None):
                    w("w_lo", b + 2)
                    take(u)
                    n = len(rhs_h)
                    for k in range(n):
                        if ready:
                            ready(k)
                        for i, (a, c) in enumerate(PASSES):
                            wt = (whi if a == "h" else wlo)[b % 2][:, woff + 128 * k:woff + 128 * k + 128]
                            r = (rhs_h if c == "h" else rhs_l)[k]
                            for q in range(3):
                                mm = nc.tensor.matmul(dst(q), wt, r(q), start=(k == 0 and i == 0), stop=(k == n - 1 and i == 2))
                    mm.then_inc(S["mm"], 1)

                def tok(tile):
                    return lambda q: tile[:, q * CH:(q + 1) * CH]

                def to_slot(u):
                    return lambda q: ps[:, 3 * (u % 2) + q, 0:CH]

                def norm_sum(u, tile):
                    take(u)
                    for q in range(3):
                        mm = nc.tensor.matmul(ps[:, 3 * (u % 2) + q, 0:CH], ones[:, :], tile[:, q * CH:(q + 1) * CH], start=True, stop=True)
                    mm.then_inc(S["mm"], 1)

                pe.wait_ge(S["const_in"], 64)
                pe.wait_ge(S["sq_sum"], L * 7 + 7)
                norm_sum(U_SMIX, msq)
                XH, XL = [tok(t) for t in xgh], [tok(t) for t in xgl]
                pe.wait_ge(S["xg_lo"], L * 8 + 8)

                def gates(c):
                    w("xc_lo", c + 1)
                    for k in range(2):
                        product(to_slot(U_GATE[c] + k), U_GATE[c] + k, B_GATE[c], 128 * k, [tok(xch)], [tok(xcl)])

                for c in range(4):
                    product(to_slot(U_XR[c]), U_XR[c], B_XR[c], 0, XH, XL)
                gates(0)
                for c in (0, 1):
                    product(to_slot(U_GR[c]), U_GR[c], B_GR[c], 0, XH, XL)
                gates(1)
                for c in (2, 3):
                    product(to_slot(U_GR[c]), U_GR[c], B_GR[c], 0, XH, XL)
                gates(2)
                for c in (0, 1):
                    product(to_slot(U_CKV[c]), U_CKV[c], B_CKV[c], 0, XH, XL)
                gates(3)
                product(to_slot(U_KR), U_KR, B_KR, 0, XH, XL)
                product(to_slot(U_CQ[0]), U_CQ[0], B_CQ[0], 0, XH, XL)
                w("ckv_sum", 1)
                norm_sum(U_SKV, sqa)
                for c in range(1, 6):
                    product(to_slot(U_CQ[c]), U_CQ[c], B_CQ[c], 0, XH, XL)
                for m in range(6):
                    product(to_slot(U_UQ[m]), U_UQ[m], B_UQ + m, 0, [tok(t) for t in cqh], [tok(t) for t in cql],
                            (lambda k: w("cq_lo", k + 1)) if m == 0 else None)
                    if m == 0:
                        w("cq_sum", 5)
                        norm_sum(U_SQ, sqa)
                w("y_sum", 3)
                norm_sum(U_SY, t3)
                w("w_lo", B_UV + 2)
                w("ckv_lo", 2)
                for t in range(10):
                    u = U_V + t
                    take(u)
                    c0 = VTILES[t]
                    for k in range(2):
                        for i, (a, c) in enumerate((("h", "h"), ("h", "l"), ("l", "h"))):
                            mm = nc.tensor.matmul(ps[:, 3 * (u % 2), :], (ckvh if a == "h" else ckvl)[k][:, c0:c0 + P],
                                                  (whi if c == "h" else wlo)[B_UV % 2][:, 512 * k:512 * k + 512],
                                                  start=(k == 0 and i == 0), stop=(k == 1 and i == 2))
                    mm.then_inc(S["mm"], 1)
                for j in range(4):
                    product(lambda q: ps[:, 3 * ((U_K + j) % 2) + q, 0:KCH], U_K + j, B_UK, 256 * j,
                            [(lambda q, t=t: t[:, q * KCH:(q + 1) * KCH]) for t in ckvh],
                            [(lambda q, t=t: t[:, q * KCH:(q + 1) * KCH]) for t in ckvl])

                take(U_K + 4)
                take(U_K + 5)

                def max_step(h, s):
                    e = h % 2
                    rows = slice(0, MAX_ROWS[e])
                    if h or s:
                        w("mxred", h * NMX + s)
                    if s == 0:
                        w("q_hi", h + 1)
                        if h >= 1:
                            w("mxt", h)
                            w("mt_lo", h)
                    for bank, q0, k0, n in MAXES[s][0]:
                        mm = nc.tensor.matmul(ps[:, 3 + bank, 0:n], qs[e][0][rows, q0:q0 + P], ks[e][0][rows, k0:k0 + n], start=True, stop=True)
                    mm.then_inc(S["mxmm"], 1)

                def max_rows(h):
                    w("mxc", h + 1)
                    nc.tensor.transpose(ps[:, 3, 0:P], mx[:, :], ident[:, :]).then_inc(S["mxt"], 1)

                w("kslot_hi", 1)
                for s in range(NMX):
                    max_step(0, s)
                max_rows(0)
                w("slot_const", 1)
                w("kslot_lo", 2)
                for gi in range(NH * NP + LAG):
                    h, i = divmod(gi, NP)
                    e = h % 2
                    if h < NH:
                        rows = slice(0, ALL_ROWS[e])
                        _, k0, _, q0, n, _ = PAIRS[i]
                        if i == 0:
                            w("aug", 16 * 6 * (h + 1))
                            w("q_lo", h + 1)
                        if gi >= 3:
                            w("p", gi - 2)
                        for j, (a, c) in enumerate(PASSES):
                            mm = nc.tensor.matmul(ps[:, gi % 3, 0:n], ks[e][0 if a == "h" else 1][rows, k0:k0 + P],
                                                  qs[e][0 if c == "h" else 1][rows, q0:q0 + n], start=(j == 0), stop=(j == 2))
                        mm.then_inc(S["s"], 1)
                    if h + 1 < NH:
                        if i in MX_AT:
                            max_step(h + 1, MX_AT.index(i))
                        if i == MX_END + 1:
                            max_rows(h + 1)
                    if gi >= LAG:
                        gk = gi - LAG
                        hk, k = divmod(gk, NP)
                        kt, _, n_rows, q0, n, _ = PAIRS[k]
                        bank, c0 = o_place(q0)
                        _, hi, lo = p_buffers(gk)
                        w("p_lo", gk + 1)
                        if k in (0, 2) and hk >= 1:
                            w("o_ev", 2 * hk - 1 + k // 2)
                            w("s_ev", 2 * hk - 1 + k // 2)
                        v0 = VW * kt + 65 * hk
                        for j, (v, p) in enumerate(((vh, hi), (vl, hi), (vh, lo))):
                            mm = nc.tensor.matmul(ps[0:65, bank, c0:c0 + n], v[0:n_rows, v0:v0 + 65], p[0:n_rows, 0:n],
                                                  start=(k in FIRST and j == 0), stop=(k in LAST and j == 2))
                        mm.then_inc(S["pv"], 1)

                w("o_ev", 2 * NH)
                w("s_ev", 2 * NH)
                w("mxt", NH)
                w("mt_lo", NH)
                for bi, ms in enumerate(OY_TILES):
                    for n, m in enumerate(ms):
                        i = OY_ORDER.index(m)
                        if i == 3:
                            w("o_sum", 3)
                            norm_sum(U_SO, osq)
                        product(to_slot(U_OY[i]), U_OY[i], B_OY + bi, 512 * n, [tok(t) for t in yh], [tok(t) for t in yl],
                                (lambda k: w("y_lo", k + 1)) if i == 0 else None)
                for m in range(8):
                    product(to_slot(U_OO + m), U_OO + m, B_OO + m // 2, 512 * (m % 2), [tok(t) for t in oh], [tok(t) for t in ol],
                            (lambda k: w("o_lo", k + 1)) if m == 0 else None)

                w("xm_sum", 7)
                norm_sum(U_SMLP, msq)
                w("root", 6)
                wait_alone(pe, "res_add", L * PER["res_add"] + 8)
                w("xm_lo", 8)
                MH, ML = [tok(t) for t in xmh], [tok(t) for t in xml]
                FH, FL = [tok(t) for t in fh], [tok(t) for t in fl]
                with pe.Fori(0, GROUPS) as gg:
                    for k in range(2 * GT):
                        u, b = U_MLP + k, B_MLP + k
                        pe.wait_ge(S["w_lo"], L * NB + gg * (2 * GT) + (b + 2))
                        if k < 2:
                            pe.wait_ge(S["res_add"], L * PER["res_add"] + gg * 8 + (7 + k))
                        else:
                            name, j = ("relu", k - 1) if k < GT + 2 else ("res_add", 8 + k - 2 - GT + 1)
                            pe.wait_ge(S[name], L * PER[name] + gg * 8 + j)
                        rh, rl = (MH, ML) if k < GT else (FH, FL)
                        for kk in range(8):
                            if k == GT:
                                pe.wait_ge(S["f_lo"], L * PER["f_lo"] + gg * GT + (kk + 1))
                            for i, (a, c) in enumerate(PASSES):
                                wt = (whi if a == "h" else wlo)[b % 2][:, 128 * kk:128 * kk + 128]
                                for q in range(3):
                                    mm = nc.tensor.matmul(ps[:, 3 * (u % 2) + q, 0:CH], wt, (rh if c == "h" else rl)[kk](q),
                                                          start=(kk == 0 and i == 0), stop=(kk == 7 and i == 2))
                        mm.then_inc(S["mm"], 1)

            pe.wait_ge(S["sq_sum"], DEPTH * 7 + 7)
            pe.wait_ge(S["res_add"], DEPTH * PER["res_add"])
            for q in range(3):
                mm = nc.tensor.matmul(ps[:, q, 0:CH], ones[:, :], msq[:, q * CH:(q + 1) * CH], start=True, stop=True)
            mm.then_inc(S["mm"], 1)

        @block.scalar
        def _(act):
            act.dma_start(vecs[:, :], vec[0]).then_inc(S["const_in"], 16)
            act.wait_ge(S["const_in"], 64)
            for m in range(8):
                act.wait_ge(S[f"x_load{m}"], 16)
                nc.scalar.activation(xgh[m][:, :], x[m], ACT.Copy, scale=col(V_GMIX + m)).then_inc(S["xg_hi"], 1)
                if m >= 2:
                    act.wait_ge(S["sq_sum"], m - 1)
                nc.scalar.activation((rs if m else msq)[:, :], x[m], ACT.Square).then_inc(S["sq"], 1)
            act.wait_ge(S["const_set"], 1)
            with act.Fori(0, DEPTH) as L:
                def w(name, k):
                    assert k > 0, name
                    act.wait_ge(S[name], L * PER[name] + k)

                def split(b):
                    w(f"raw{b % 2}", 16 * (b // 2 + 1))
                    if b >= 2:
                        w("mm", LAST_UNIT[b - 2] + 1)
                    n = WCOLS[b]
                    nc.scalar.activation(whi[b % 2][:, 0:n], raw[b % 2][:, 0:n], ACT.Copy).then_inc(S["w_hi"], 1)

                def root(u, dst, dim):
                    w("mm", u + 1)
                    nc.scalar.activation(chunks(dst), slot(u), ACT.Sqrt, scale=1.0 / dim, bias=eps[:, 0:1]).then_inc(S["root"], 1)

                def xc_hi(c):
                    w("conv", c + 1)
                    if c:
                        w("mm", U_GATE[c - 1] + 2)
                    nc.scalar.activation(xch[:, :], xc[c][:, :], ACT.Copy).then_inc(S["xc_hi"], 1)

                def gates(c):
                    w("mm", U_GATE[c] + 1)
                    if c:
                        w("hid", c)
                    else:
                        w("conv", 4)
                    nc.scalar.activation(chunks(t1), slot(U_GATE[c]), ACT.Tanh, scale=0.5, bias=half_ba[:, c:c + 1]).then_inc(S["gate_r"], 1)
                    w("gate_r", c + 1)
                    nc.scalar.activation(t1[:, :], t1[:, :], ACT.Tanh, scale=sp2[:, c:c + 1], bias=sp2[:, c:c + 1]).then_inc(S["gate_t"], 1)
                    w("mm", U_GATE[c] + 2)
                    nc.scalar.activation(chunks(t4), slot(U_GATE[c] + 1), ACT.Tanh, scale=0.5, bias=half_bx[:, c:c + 1]).then_inc(S["gate_i"], 1)
                    w("gate_t", c + 1)
                    nc.scalar.activation(t3[:, :], t1[:, :], ACT.Sqrt).then_inc(S["root_t"], 1)

                def gelu_a(c):
                    w("gr_ev", c + 1)
                    w("lru_w", c + 1)
                    nc.scalar.activation(t2[:, :], g[c][:, :], ACT.Square).then_inc(S["g_sq"], 1)

                def gelu_b(c):
                    w("g_cube", c + 1)
                    nc.scalar.activation(t2[:, :], t2[:, :], ACT.Tanh, scale=GELU_C).then_inc(S["g_tanh"], 1)

                split(0)
                root(U_SMIX, rs, DM)
                split(1)
                w("vec_in", 64)
                w("spw_abs", 1)
                nc.scalar.activation(spw[:, 4:8], spw[:, 0:4], ACT.Exp, scale=-1.0).then_inc(S["spw_exp"], 1)
                split(2)
                split(3)
                xc_hi(0)
                w("sp2", 1)
                split(4)
                split(5)
                gates(0)
                split(6)
                xc_hi(1)
                split(7)
                gelu_a(0)
                split(8)
                gelu_b(0)
                gates(1)
                split(9)
                xc_hi(2)
                split(10)
                gelu_a(1)
                split(11)
                gelu_b(1)
                gates(2)
                split(12)
                xc_hi(3)
                split(13)
                gelu_a(2)
                split(14)
                gelu_b(2)
                gates(3)
                split(15)
                split(16)
                gelu_a(3)
                w("mm", U_GATE[3] + 2)
                for c in range(2):
                    w("ckv_ev", c + 1)
                    nc.scalar.activation((sqt if c else sqa)[:, :], ckv[c][:, 0:T], ACT.Square).then_inc(S["ckv_sq"], 1)
                gelu_b(3)
                split(17)
                root(U_SKV, sqt, KVL)

                def cq_square(c):
                    w("cq_ev", c + 1)
                    if c == 1:
                        w("ckv_n", 2)
                    if c >= 2:
                        w("cq_sum", c - 1)
                    nc.scalar.activation((sqt if c else sqa)[:, :], cq[c][:, :], ACT.Square).then_inc(S["cq_sq"], 1)

                cq_square(0)
                split(18)
                cq_square(1)
                split(19)
                cq_square(2)
                cq_square(3)
                split(20)
                cq_square(4)
                split(21)
                w("mm", U_CQ[5] + 1)
                for c in range(6):
                    if c == 1:
                        cq_square(5)
                    nc.scalar.activation(cqh[c][:, :], cq[c][:, :], ACT.Copy, scale=col(V_QG + c)).then_inc(S["cq_hi"], 1)
                split(22)
                w("ckv_full", 1)
                for c in range(2):
                    nc.scalar.activation(ckvh[c][:, :], ckv[c][:, :], ACT.Copy).then_inc(S["ckv_hi"], 1)
                def queries_out(c):
                    w("mm", U_UQ[c] + 1)
                    w("cq_lo", 6)
                    nc.scalar.activation(chunks(qn[c]), slot(U_UQ[c]), ACT.Copy).then_inc(S["qn_raw"], 1)

                queries_out(0)
                w("cq_ev", 6)
                root(U_SQ, rs, QL)
                split(23)
                queries_out(1)
                split(24)
                for c in range(4):
                    w("y", 4)
                    if c >= 2:
                        w("y_sum", c - 1)
                    nc.scalar.activation((t4[:, 0:T] if c else t3[:, :]), g[c][:, :], ACT.Square).then_inc(S["y_sq"], 1)
                for b in (25, 26, 27):
                    split(b)
                w("qr_ev", 2)
                root(U_SY, rs, LRU)
                split(28)
                w("v_one", 1)
                for t in range(10):
                    w("mm", U_V + t + 1)
                    dst = vh[:, VW * t:VW * (t + 1)].rearrange("p (h d) -> p h d", h=NH)[:, :, 0:64]
                    nc.scalar.activation(dst, ps[:, 3 * ((U_V + t) % 2), :].rearrange("p (h d) -> p h d", h=NH), ACT.Copy)\
                        .then_inc(S["v_hi"], 1)
                w("cq_lo", 6)
                for j in range(4):
                    w("mm", U_K + j + 1)
                    b0 = 3 * ((U_K + j) % 2)
                    nc.scalar.activation(kf[j][:, :].rearrange("p (c n) -> p c n", c=3), ps[:, b0:b0 + 3, 0:KCH], ACT.Copy).then_inc(S["kf"], 1)

                w("kpe", 16 * 8)
                for e in range(2):
                    nc.scalar.activation(ks[e][0][PE_ROWS[e], :], kpe[PE_ROWS[e], :], ACT.Copy).then_inc(S["kslot_hi"], 1)
                split(29)
                split(30)

                def shift_hi(h):
                    w("mxt", h + 1)
                    if h:
                        w("aug", 16 * 6 * h)
                    nc.scalar.activation(mth[0:10, :], ps[0:10, 3, 0:P], ACT.Copy, scale=-1.0).then_inc(S["mt_hi"], 1)

                def o_out(h):
                    w("pv", (h + 1) * NP)
                    d, r = o[h // 2], half(h % 2)
                    nc.scalar.activation(d[r, 0:272], ps[0:64, 5, 0:272], ACT.Copy)
                    nc.scalar.activation(d[r, STREAM:TOK], ps[0:64, 5, 272:272 + DEC], ACT.Copy).then_inc(S["o_ev"], 1)
                    nc.scalar.activation(d[r, 272:STREAM].rearrange("p (a n) -> p a n", a=2), ps[0:64, 6:8, 0:384], ACT.Copy).then_inc(S["o_ev"], 1)

                shift_hi(0)
                w("row_set", 12)
                for gi in range(NH * NP):
                    h, i = divmod(gi, NP)
                    _, _, rows, _, n, diag = PAIRS[i]
                    whole, hi, _ = p_buffers(gi)
                    w("s", gi + 1)
                    if PH_BEFORE[gi] is not None:
                        w("pv", PH_BEFORE[gi] + 1)
                    if P32_BEFORE[gi] is not None:
                        w("p_lo", P32_BEFORE[gi] + 1)
                    src = ps[:, gi % 3, :]
                    for dst in (hi, whole):
                        if diag:
                            nc.scalar.activation(dst[0:64, 0:64], src[0:64, 0:64], ACT.Exp, scale=SM_SCALE)
                            ins = nc.scalar.activation(dst[:, 64:n], src[:, 64:n], ACT.Exp, scale=SM_SCALE)
                        else:
                            ins = nc.scalar.activation(dst[0:rows, 0:n], src[0:rows, 0:n], ACT.Exp, scale=SM_SCALE)
                    ins.then_inc(S["p"], 1)
                    if i == LAG - 1 and h >= 1:
                        o_out(h - 1)
                    if i == MX_END + 1 and h + 1 < NH:
                        shift_hi(h + 1)
                o_out(NH - 1)
                for m in range(5):
                    act.dma_start(x[m], x_scr[m]).then_inc(S[f"x_in{m}"], 16)

                for c in range(4):
                    if c == 0:
                        w("y_n", 4)
                    nc.scalar.activation(yh[c][:, :], g[c][:, :], ACT.Copy, scale=col(V_LG + c)).then_inc(S["y_hi"], 1)
                for j in range(4):
                    if j == 3:
                        split(31)
                    w("o", j + 1)
                    if j >= 2:
                        w("o_sum", j - 1)
                    nc.scalar.activation((osqt if j else osq)[:, :], o[j][:, :], ACT.Square).then_inc(S["o_sq"], 1)
                root(U_SO, rs, ATT)
                split(32)
                for j in range(4):
                    w("o_n", j + 1)
                    nc.scalar.activation(oh[j][:, :], o[j][:, :], ACT.Copy, scale=col(V_AG + j)).then_inc(S["o_hi"], 1)
                split(33)
                split(34)
                split(35)
                for m in range(8):
                    if m and m % 2 == 0:
                        split(35 + m // 2)
                    w("res_add", m + 1)
                    nc.scalar.activation(xmh[m][:, :], x[m], ACT.Copy, scale=col(V_MG + m)).then_inc(S["xm_hi"], 1)
                    if m >= 2:
                        w("xm_sum", m - 1)
                    nc.scalar.activation((rs if m else msq)[:, :], x[m], ACT.Square).then_inc(S["xm_sq"], 1)
                split(B_MLP + 1)
                w("xm_sum", 7)
                root(U_SMLP, rs, DM)

                def mlp_group(gg, last):
                    for k in range(2 * GT):
                        if not (last and k >= 2 * GT - 2):
                            b = B_MLP + k + 2
                            act.wait_ge(S["mm"], L * NU + gg * (2 * GT) + (U_MLP + k + 1))
                            act.wait_ge(S[f"raw{b % 2}"], L * PER["raw0"] + gg * (16 * GT) + 16 * (b // 2 + 1))
                            nc.scalar.activation(whi[b % 2][:, :], raw[b % 2][:, :], ACT.Copy).then_inc(S["w_hi"], 1)
                        if k < GT:
                            act.wait_ge(S["relu"], L * PER["relu"] + gg * GT + (k + 1))
                            nc.scalar.activation(msq[:, :], msq[:, :], ACT.Square).then_inc(S["f_sq"], 1)
                            act.wait_ge(S["f_sq"], L * PER["f_sq"] + gg * GT + (k + 1))
                            nc.scalar.activation(fh[k][:, :], msq[:, :], ACT.Copy).then_inc(S["f_hi"], 1)
                        elif last:
                            m = k - GT
                            w("res_add", GROUPS * 8 + m + 1)
                            nc.scalar.activation(xgh[m][:, :], x[m], ACT.Copy, scale=col(V_GNEXT + m)).then_inc(S["xg_hi"], 1)
                            if m >= 2:
                                act.wait_ge(S["sq_sum"], L * 7 + 7 + (m - 1))
                            nc.scalar.activation((rs if m else msq)[:, :], x[m], ACT.Square).then_inc(S["sq"], 1)

                with act.Fori(0, GROUPS - 1) as gg:
                    mlp_group(gg, False)
                mlp_group(GROUPS - 1, True)
            act.wait_ge(S["mm"], DEPTH * NU + 1)
            act.wait_ge(S["sq_sum"], DEPTH * 7 + 7)
            nc.scalar.activation(chunks(rs), ps[:, 0:3, 0:CH], ACT.Sqrt, scale=1.0 / DM, bias=eps[:, 0:1]).then_inc(S["root"], 1)

        @block.vector
        def _(dve):
            V = nc.vector
            V.memset(eps[:, :], EPS).then_inc(S["w_lo"], 1)
            V.memset(mx[:, :], 0.0).then_inc(S["const_set"], 1)
            dve.wait_ge(S["const_in"], 64)
            for m in range(8):
                dve.wait_ge(S["xg_hi"], m + 1)
                V.scalar_tensor_tensor(out=xgl[m][:, :], in0=x[m], scalar=col(V_GMIX + m), in1=xgh[m][:, :].bitcast(F32),
                                       op0=ALU.mult, op1=ALU.subtract).then_inc(S["xg_lo"], 1)
                if m:
                    dve.wait_ge(S["sq"], m + 1)
                    if m > 1:
                        dve.wait_ge(S["sq_sum"], m - 1)
                    V.tensor_tensor(msq[:, :], msq[:, :], rs[:, :], ALU.add).then_inc(S["sq_sum"], 1)
            chain = [0]
            with dve.Fori(0, DEPTH) as L:
                def w(name, k):
                    assert k > 0, name
                    dve.wait_ge(S[name], L * PER[name] + k)

                def link(ins):
                    chain[0] += 1
                    ins.then_inc(S["dve_chain"], 1)
                    w("dve_chain", chain[0])

                def split(b):
                    w("w_hi", b + 1)
                    n = WCOLS[b]
                    V.tensor_tensor(wlo[b % 2][:, 0:n], raw[b % 2][:, 0:n], whi[b % 2][:, 0:n].bitcast(F32), ALU.subtract).then_inc(S["w_lo"], 1)

                def rstd(dst, n):
                    w("root", n)
                    V.reciprocal(dst[:, :], dst[:, :]).then_inc(S["rstd"], 1)
                    w("rstd", n)

                def scaled(u, dst, by, name):
                    w("mm", u + 1)
                    V.tensor_tensor(chunks(dst), slot(u), chunks(by), ALU.mult).then_inc(S[name], 1)

                def lo(dst, src, hi, name, gain=None):
                    if gain is None:
                        V.tensor_tensor(dst, src, hi.bitcast(F32), ALU.subtract).then_inc(S[name], 1)
                    else:
                        V.scalar_tensor_tensor(out=dst, in0=src, scalar=gain, in1=hi.bitcast(F32), op0=ALU.mult, op1=ALU.subtract)\
                            .then_inc(S[name], 1)

                def conv(c, block=None):
                    scaled(U_XR[c], t4[:, CW - 1:CW - 1 + T], rs, "xr_ev")
                    if block is not None:
                        split(block)
                    w("xr_ev", c + 1)
                    link(V.tensor_copy(xs[:, c, CW - 1:], t4[:, CW - 1 + STREAM:CW - 1 + T]))
                    V.tensor_copy(cbuf[:, c, 0, :], t4[:, STREAM:STREAM + CW - 1])
                    V.tensor_copy(cbuf[:, c, 1, :], t4[:, TOK:TOK + CW - 1])
                    for src, n, dst in ((t4[:, :], STREAM, xc[c][:, 0:STREAM]), (xs[:, c, :], DEC + 2, xc[c][:, STREAM:T])):
                        link(V.tensor_scalar(dst, src[:, 3:3 + n], col(V_CW + 4 * c + 3), col(V_CB + c), ALU.mult, ALU.add))
                        for k in (2, 1, 0):
                            ins = V.scalar_tensor_tensor(out=dst, in0=src[:, k:k + n], scalar=col(V_CW + 4 * c + k), in1=dst,
                                                         op0=ALU.mult, op1=ALU.add)
                            if k or n == STREAM:
                                link(ins)
                    ins.then_inc(S["conv"], 1)

                def xc_lo(c):
                    w("xc_hi", c + 1)
                    lo(xcl[:, :], xc[c][:, :], xch[:, :], "xc_lo")

                def lru(c):
                    w("gate_t", c + 1)
                    link(V.tensor_scalar(t2[:, :], t1[:, :], 1.0, None, ALU.add))
                    link(V.reciprocal(t2[:, :], t2[:, :]))
                    w("root_t", c + 1)
                    V.tensor_scalar(t1[:, :], t2[:, :], 2.0, -1.0, ALU.mult, ALU.add)
                    V.scalar_tensor_tensor(out=t3[:, :], in0=t3[:, :], scalar=2.0, in1=t2[:, :], op0=ALU.mult, op1=ALU.mult).then_inc(S["lru_w"], 1)
                    w("gate_i", c + 1)
                    link(V.scalar_tensor_tensor(out=t4[:, 0:T], in0=t4[:, 0:T], scalar=1.0, in1=xc[c][:, :], op0=ALU.add, op1=ALU.mult))
                    link(V.scalar_tensor_tensor(out=t4[:, 0:T], in0=t4[:, 0:T], scalar=0.5, in1=t3[:, :], op0=ALU.mult, op1=ALU.mult))
                    V.tensor_tensor_scan(xc[c][:, 0:STREAM], t1[:, 0:STREAM], t4[:, 0:STREAM], 0.0, ALU.mult, ALU.add)
                    V.tensor_tensor_scan(xc[c][:, STREAM:T], t1[:, STREAM:T], t4[:, STREAM:T], h0s[:, c:c + 1], ALU.mult, ALU.add)\
                        .then_inc(S["hid"], 1)
                    w("hid", c + 1)
                    V.tensor_copy(hbuf[:, c, 0:1], xc[c][:, STREAM - 1:STREAM])
                    link(V.tensor_copy(hbuf[:, c, 1:2], xc[c][:, TOK - 1:TOK]))

                def gelu(c):
                    w("g_tanh", c + 1)
                    link(V.scalar_tensor_tensor(out=g[c][:, :], in0=t2[:, :], scalar=1.0, in1=g[c][:, :], op0=ALU.add, op1=ALU.mult))
                    V.scalar_tensor_tensor(out=g[c][:, :], in0=g[c][:, :], scalar=0.5, in1=xc[c][:, :], op0=ALU.mult, op1=ALU.mult)\
                        .then_inc(S["y"], 1)

                HALF_SWAP = list(range(16, 32)) + list(range(16))

                def rotate(buf, tmp, name):
                    link(V.stream_shuffle(tmp, buf, HALF_SWAP))
                    link(V.tensor_tensor(tmp, tmp, sinT[:, :], ALU.mult))
                    link(V.tensor_tensor(buf, buf, cosT[:, :], ALU.mult))
                    V.tensor_tensor(buf, buf, tmp, ALU.add).then_inc(S[name], 1)

                split(0)
                rstd(rs, 1)
                split(1)
                w("vec_in", 64)
                lam = vecs[:, V_LAM:V_LAM + 4]
                V.tensor_scalar(half_ba[:, :], vecs[:, V_BA:V_BA + 4], 0.5, None, ALU.mult)
                V.tensor_scalar(half_bx[:, :], vecs[:, V_BX:V_BX + 4], 0.5, None, ALU.mult)
                link(V.tensor_scalar(sp2[:, :], lam, -1.0, 0.0, ALU.mult, ALU.max))
                V.scalar_tensor_tensor(out=spw[:, 0:4], in0=sp2[:, :], scalar=2.0, in1=lam, op0=ALU.mult, op1=ALU.add).then_inc(S["spw_abs"], 1)
                w("spw_exp", 1)
                e_, s_, s2, p_ = spw[:, 4:8], spw[:, 0:4], spw[:, 8:12], spw[:, 12:16]
                link(V.tensor_scalar(s2, e_, 2.0, None, ALU.add))
                link(V.reciprocal(s2, s2))
                link(V.tensor_tensor(s_, e_, s2, ALU.mult))
                link(V.tensor_tensor(s2, s_, s_, ALU.mult))
                link(V.tensor_scalar(p_, s2, 1.0 / 19, None, ALU.mult))
                for d in (17, 15, 13, 11, 9, 7, 5, 3):
                    link(V.scalar_tensor_tensor(out=p_, in0=p_, scalar=1.0 / d, in1=s2, op0=ALU.add, op1=ALU.mult))
                link(V.scalar_tensor_tensor(out=p_, in0=p_, scalar=1.0, in1=s_, op0=ALU.add, op1=ALU.mult))
                link(V.tensor_scalar(sp2[:, :], sp2[:, :], 2.0, None, ALU.mult))
                V.scalar_tensor_tensor(out=sp2[:, :], in0=p_, scalar=4.0, in1=sp2[:, :], op0=ALU.mult, op1=ALU.add).then_inc(S["sp2"], 1)

                dve.wait_ge(S["x_out"], L * 128 + 128)
                dve.wait_ge(S["sq"], L * 8 + 8)
                dve.wait_ge(S["xg_lo"], L * 8 + 8)
                link(V.memset(t4[:, 0:CW - 1], 0.0))
                conv(0)
                split(2)
                conv(1)
                split(3)
                xc_lo(0)
                conv(2)
                split(4)
                conv(3, 5)
                split(6)
                xc_lo(1)
                lru(0)
                split(7)
                scaled(U_GR[0], g[0], rs, "gr_ev")
                scaled(U_GR[1], g[1], rs, "gr_ev")
                split(8)
                gelu(0)
                split(9)
                xc_lo(2)
                lru(1)
                split(10)
                scaled(U_GR[2], g[2], rs, "gr_ev")
                scaled(U_GR[3], g[3], rs, "gr_ev")
                split(11)
                gelu(1)
                split(12)
                xc_lo(3)
                lru(2)
                split(13)
                scaled(U_CKV[0], ckv[0][:, 0:T], rs, "ckv_ev")
                scaled(U_CKV[1], ckv[1][:, 0:T], rs, "ckv_ev")
                split(14)
                gelu(2)
                split(15)
                lru(3)
                scaled(U_KR, kpe[:, 0:T], rs, "kr_ev")
                split(16)
                scaled(U_CQ[0], cq[0], rs, "cq_ev")
                gelu(3)
                wait_alone(dve, "table_in", L * PER["table_in"] + 32)
                w("kr_ev", 1)
                rotate(kpe[:, 0:T], t1[:, :], "kpe_new")
                split(17)
                rstd(sqt, 2)
                for c in range(2):
                    V.scalar_tensor_tensor(out=ckv[c][:, 0:T], in0=ckv[c][:, 0:T], scalar=col(V_KVG + c), in1=sqt[:, :], op0=ALU.mult, op1=ALU.mult)\
                        .then_inc(S["ckv_n"], 1)
                w("ckv_n", 2)
                scaled(U_CQ[1], cq[1], rs, "cq_ev")
                for c in range(2):
                    V.tensor_copy(ckv[c][:, PAST_A:META2], past[:, c, 0:96])
                    V.tensor_copy(ckv[c][:, META2:PAST_B], ckv[c][:, 0:NMETA])
                    V.tensor_copy(ckv[c][:, PAST_B:KEY_END], past[:, c, 96:PAST])
                    ins = V.memset(ckv[c][:, KEY_END:KW], 0.0)
                ins.then_inc(S["ckv_full"], 1)
                w("kpe_new", 1)
                V.memset(kpe[:, KEY_END:KW], 0.0)
                V.tensor_copy(kpe[:, META2:PAST_B], kpe[:, 0:NMETA]).then_inc(S["kpe_meta"], 1)
                split(18)
                scaled(U_CQ[2], cq[2], rs, "cq_ev")
                split(19)
                scaled(U_CQ[3], cq[3], rs, "cq_ev")
                split(20)
                scaled(U_CQ[4], cq[4], rs, "cq_ev")
                split(21)
                V.tensor_copy(hbuf[:, 3, 1:2], xc[3][:, TOK - 1:TOK]).then_inc(S["hid_out"], 1)
                for c in range(6):
                    w("cq_hi", c + 1)
                    lo(cql[c][:, :], cq[c][:, :], cqh[c][:, :], "cq_lo", col(V_QG + c))
                    if c == 0:
                        scaled(U_CQ[5], cq[5], rs, "cq_ev")
                split(22)
                w("kv_out", 32)
                for c in range(2):
                    w("ckv_hi", c + 1)
                    lo(ckvl[c][:, :], ckv[c][:, :], ckvh[c][:, :], "ckv_lo")
                split(23)
                rstd(rs, 3)
                split(24)
                for c in range(2):
                    w("qn_raw", c + 1)
                    V.tensor_tensor(qn[c][:, :], qn[c][:, :], rs[:, :], ALU.mult).then_inc(S["qn"], 1)
                scaled(U_UQ[2], qn[2], rs, "qn")
                split(25)
                scaled(U_UQ[3], qn[3], rs, "qn")
                split(26)
                scaled(U_UQ[4], qr[0], rs, "qr_ev")
                wait_alone(dve, "qr_ev", L * PER["qr_ev"] + 1)
                rotate(qr[0][:, :], rtmp[:, :], "qr")
                split(27)
                scaled(U_UQ[5], qr[1], rs, "qr_ev")
                w("y_sum", 3)
                w("mm", U_SY + 1)
                V.memset(vh[:, :].bitcast(F32).rearrange("p (t d) -> p t d", d=65)[:, :, 64:65], 1.0)
                V.memset(vl[:, :].bitcast(F32).rearrange("p (t d) -> p t d", d=65)[:, :, 64:65], 0.0).then_inc(S["v_one"], 1)
                split(28)
                for t in range(10):
                    w("v_hi", t + 1)
                    hi = vh[:, VW * t:VW * (t + 1)].rearrange("p (h d) -> p h d", h=NH)[:, :, 0:64]
                    dst = vl[:, VW * t:VW * (t + 1)].rearrange("p (h d) -> p h d", h=NH)[:, :, 0:64]
                    V.tensor_tensor(dst, ps[:, 3 * ((U_V + t) % 2), :].rearrange("p (h d) -> p h d", h=NH), hi.bitcast(F32), ALU.subtract)\
                        .then_inc(S["v_lo"], 1)
                wait_alone(dve, "qr_ev", L * PER["qr_ev"] + 2)
                w("qr", 1)
                rotate(qr[1][:, :], rtmp[:, :], "qr")
                rstd(rs, 4)
                for c in range(4):
                    V.tensor_tensor(g[c][:, :], g[c][:, :], rs[:, :], ALU.mult).then_inc(S["y_n"], 1)


                def slot_parts(h):
                    j, e = h // 2, h % 2
                    return (qs[e], qn[j], half(e)), (qs[e], ra[j], PE_ROWS[e]), (ks[e], kf[j], half(e))

                def load_hi(h):
                    if h == 0:
                        w("ra0", 64)
                        w("qn", 4)
                        w("kf", 4)
                    if h == 4:
                        w("ra1", 64)
                    if h >= 2:
                        w("s", (h - 1) * NP)
                    if h % 2 == 1 and h >= 3:
                        V.memset(qs[1][0][32:33, :].bitcast(F32), 0.0)
                    for dst, src, rows in slot_parts(h):
                        ins = V.tensor_copy(dst[0][rows, :], src[rows, :])
                    ins.then_inc(S["q_hi"], 1)

                def load_lo(h, part):
                    dst, src, rows = slot_parts(h)[part]
                    if part == 0:
                        w("q_hi", h + 1)
                    ins = V.tensor_tensor(dst[1][rows, :], src[rows, :], dst[0][rows, :].bitcast(F32), ALU.subtract)
                    if part == 2:
                        ins.then_inc(S["q_lo"], 1)

                def reduce_max(h, s):
                    w("mxmm", h * NMX + s + 1)
                    if s == 0 and h:
                        w("mxt", h)
                    for lo_, hi_, c0, n, second, c in MAXES[s][1]:
                        dst = (mx2 if second else mx)[lo_:hi_, c:c + 1]
                        ins = V.reduce_max(dst, ps[lo_:hi_, 3:5, :].rearrange("p a n -> p (a n)")[:, c0:c0 + n], AX_X)
                    ins.then_inc(S["mxred"], 1)

                def both_halves(h):
                    w("mxred", (h + 1) * NMX)
                    V.tensor_tensor(mx[64:P, 0:8], mx[64:P, 0:8], mx2[64:P, :], ALU.max).then_inc(S["mxc"], 1)

                def shift_lo(h):
                    w("mt_hi", h + 1)
                    V.scalar_tensor_tensor(out=mtl[0:10, :], in0=ps[0:10, 3, 0:P], scalar=-1.0, in1=mth[0:10, :].bitcast(F32),
                                           op0=ALU.mult, op1=ALU.subtract).then_inc(S["mt_lo"], 1)

                def sums_out(h):
                    w("pv", (h + 1) * NP)
                    if h >= 2:
                        w("sum_out", 16 * (h - 1))
                    r = slice(64 * (h % 2), 64 * (h % 2) + 1)
                    V.tensor_copy(srow[r, 0:272], ps[64:65, 5, 0:272])
                    V.tensor_copy(srow[r, STREAM:TOK], ps[64:65, 5, 272:272 + DEC]).then_inc(S["s_ev"], 1)
                    V.tensor_copy(srow[r, 272:STREAM].rearrange("p (a n) -> p a n", a=2), ps[64:65, 6:8, 0:384]).then_inc(S["s_ev"], 1)

                def invert(j):
                    w("sum_in", 16 * (j + 1))
                    V.reciprocal(comp[:, :], comp[:, :]).then_inc(S["inv"], 1)

                def divide(j):
                    w("inv_in", 32 * (j + 1))
                    w("o_ev", 2 * (2 * j + 2))
                    V.memset(o[j][:, TOK:T], 0.0)
                    V.tensor_tensor(o[j][:, 0:TOK], o[j][:, 0:TOK], rc[:, 0:TOK], ALU.mult).then_inc(S["o"], 1)

                load_hi(0)
                for s in range(NMX):
                    reduce_max(0, s)
                    if s < 3:
                        load_lo(0, s)
                    if s in (3, 4):
                        w("kslot_hi", s - 2)
                        lo(ks[s - 3][1][PE_ROWS[s - 3], :], kpe[PE_ROWS[s - 3], :], ks[s - 3][0][PE_ROWS[s - 3], :], "kslot_lo")
                both_halves(0)
                shift_lo(0)
                split(29)
                split(30)
                for h in range(NH):
                    for i in range(NP):
                        if i == 0 and h + 1 < NH:
                            load_hi(h + 1)
                        if i == LAG - 1 and h >= 1:
                            sums_out(h - 1)
                        if h + 1 < NH:
                            if i in MX_AT:
                                reduce_max(h + 1, MX_AT.index(i))
                            if i == MX_END:
                                both_halves(h + 1)
                                load_lo(h + 1, 0)
                                shift_lo(h + 1)
                                load_lo(h + 1, 1)
                                load_lo(h + 1, 2)
                        if h in (2, 4, 6) and i == 8:
                            invert(h // 2 - 1)
                        if h in (3, 5, 7) and i == MX_END:
                            divide((h - 3) // 2)
                sums_out(NH - 1)

                for c in range(4):
                    w("y_hi", c + 1)
                    lo(yl[c][:, :], g[c][:, :], yh[c][:, :], "y_lo", col(V_LG + c))
                invert(3)

                def add_up(u, m, name):
                    w("mm", u + 1)
                    xm3 = x[m].rearrange("p (c n) -> p c n", c=3)
                    V.tensor_tensor(xm3, xm3, slot(u), ALU.add).then_inc(S[name], 1)

                def add_y(i):
                    w(f"x_in{OY_ORDER[i]}", 16)
                    add_up(U_OY[i], OY_ORDER[i], "oy_ev")

                add_y(0)
                divide(3)
                add_y(1)
                split(31)
                add_y(2)
                rstd(rs, 5)
                add_y(3)
                split(32)
                for j in range(4):
                    V.tensor_tensor(o[j][:, :], o[j][:, :], rs[:, :], ALU.mult).then_inc(S["o_n"], 1)
                add_y(4)
                add_y(5)
                split(33)
                for j in range(4):
                    w("o_hi", j + 1)
                    lo(ol[j][:, :], o[j][:, :], oh[j][:, :], "o_lo", col(V_AG + j))
                add_y(6)
                split(34)
                add_y(7)
                split(35)
                for m in range(8):
                    if m and m % 2 == 0:
                        split(35 + m // 2)
                    w("oy_ev", 8)
                    add_up(U_OO + m, m, "res_add")
                    w("xm_hi", m + 1)
                    lo(xml[m][:, :], x[m], xmh[m][:, :], "xm_lo", col(V_MG + m))
                split(B_MLP + 1)
                w("root", 6)
                V.reciprocal(rs[:, :], rs[:, :]).then_inc(S["rstd"], 1)
                wait_alone(dve, "rstd", L * PER["rstd"] + 6)

                def mlp_group(gg, last):
                    for k in range(2 * GT):
                        if not (last and k >= 2 * GT - 2):
                            b = B_MLP + k + 2
                            dve.wait_ge(S["w_hi"], L * NB + gg * (2 * GT) + (b + 1))
                            V.tensor_tensor(wlo[b % 2][:, :], raw[b % 2][:, :], whi[b % 2][:, :].bitcast(F32), ALU.subtract).then_inc(S["w_lo"], 1)
                        u = U_MLP + k
                        dve.wait_ge(S["mm"], L * NU + gg * (2 * GT) + (u + 1))
                        if k < GT:
                            V.scalar_tensor_tensor(out=chunks(msq), in0=slot(u), scalar=0.0, in1=chunks(rs), op0=ALU.max, op1=ALU.mult)\
                                .then_inc(S["relu"], 1)
                            dve.wait_ge(S["f_hi"], L * PER["f_hi"] + gg * GT + (k + 1))
                            V.tensor_tensor(fl[k][:, :], msq[:, :], fh[k][:, :].bitcast(F32), ALU.subtract).then_inc(S["f_lo"], 1)
                            dve.wait_ge(S["f_lo"], L * PER["f_lo"] + gg * GT + (k + 1))
                        else:
                            m = k - GT
                            if k == GT:
                                dve.wait_ge(S["res_add"], L * PER["res_add"] + gg * 8 + 8)
                            xm3 = x[m].rearrange("p (c n) -> p c n", c=3)
                            V.tensor_tensor(xm3, xm3, slot(u), ALU.add).then_inc(S["res_add"], 1)
                            if last:
                                dve.wait_ge(S["xg_hi"], L * 8 + 8 + (m + 1))
                                lo(xgl[m][:, :], x[m], xgh[m][:, :], "xg_lo", col(V_GNEXT + m))

                with dve.Fori(0, GROUPS - 1) as gg:
                    mlp_group(gg, False)
                mlp_group(GROUPS - 1, True)
            assert chain[0] == DVE_CHAIN, chain
            dve.wait_ge(S["root"], DEPTH * 6 + 1)
            dve.wait_ge(S["x_out"], DEPTH * 128 + 128)
            dve.wait_ge(S["sq"], DEPTH * 8 + 8)
            dve.wait_ge(S["xg_lo"], DEPTH * 8 + 8)
            V.reciprocal(rs[:, :], rs[:, :]).then_inc(S["rstd"], 1)
            dve.wait_ge(S["rstd"], DEPTH * 6 + 1)
            for m in range(8):
                V.scalar_tensor_tensor(out=x[m], in0=x[m], scalar=fg[:, m:m + 1], in1=rs[:, :], op0=ALU.mult, op1=ALU.mult)\
                    .then_inc(S["yout"], 1)

        @block.gpsimd
        def _(pool):
            G = nc.gpsimd

            def save_x(m):
                pool.dma_start(x_scr[m], x[m]).then_inc(S["x_out"], 16)

            for m in range(8):
                pool.wait_ge(S[f"x_load{m}"], 16)
                save_x(m)
            with pool.Fori(0, DEPTH) as L:
                def w(name, k, alone=False):
                    assert k > 0, name
                    if alone:
                        wait_alone(pool, name, L * PER[name] + k)
                    else:
                        pool.wait_ge(S[name], L * PER[name] + k)

                def sum_squares(acc, tmp, n, sq, out):
                    for m in range(1, n):
                        w(sq, m + 1)
                        if m > 1:
                            w(out, m - 1)
                        G.tensor_tensor(acc, acc, tmp, ALU.add).then_inc(S[out], 1)

                def cube(c):
                    w("g_sq", c + 1, alone=True)
                    G.tensor_scalar(t2[:, :], t2[:, :], 0.044715, 1.0, ALU.mult, ALU.add).then_inc(S["g_poly"], 1)
                    w("g_poly", c + 1)
                    G.tensor_tensor(t2[:, :], t2[:, :], g[c][:, :], ALU.mult).then_inc(S["g_cube"], 1)

                for c in range(3):
                    cube(c)
                cube(3)
                sum_squares(sqa[:, :], sqt[:, :], 2, "ckv_sq", "ckv_sum")
                w("kpe_meta", 1, alone=True)
                for q in range(4):
                    r = slice(32 * q, 32 * q + 32)
                    pool.dma_start(kpe[r, PAST_A:META2], past_kpe[L, :, 0:96]).then_inc(S["kpe"], 16)
                    pool.dma_start(kpe[r, PAST_B:KEY_END], past_kpe[L, :, 96:PAST]).then_inc(S["kpe"], 16)
                pool.dma_start(kpe_out[L], kpe[0:ROPE, 0:TOK]).then_inc(S["kpe_out"], 16)
                w("ckv_full", 1, alone=True)
                for c in range(2):
                    pool.dma_start(ckv_out[L, c], ckv[c][:, 0:TOK]).then_inc(S["kv_out"], 16)
                sum_squares(sqa[:, :], sqt[:, :], 6, "cq_sq", "cq_sum")
                w("hid_out", 1, alone=True)
                pool.dma_start(h_out[L], hbuf[:, :, :]).then_inc(S["small_out"], 16)
                pool.dma_start(conv_out[L], cbuf[:, :, :, :]).then_inc(S["small_out"], 16)
                sum_squares(t3[:, :], t4[:, 0:T], 4, "y_sq", "y_sum")

                w("kf", 4)
                w("qr", 2)
                w("ra1", 64, alone=True)
                n_row = 0
                for k in range(2):
                    for dst, value in ((pd[k][:, 0:64], 0.0), (phd[k][:, 0:64].bitcast(F32), 0.0), (ks[0][k][96:97, :].bitcast(F32), 1.0 - k),
                                       (ks[1][k][32:64, :].bitcast(F32), 0.0),
                                       (qs[0][k][96:97, :].bitcast(F32), 0.0), (qs[1][k][32:64, :].bitcast(F32), 0.0)):
                        G.memset(dst, value).then_inc(S["row_set"], 1)
                        n_row += 1
                        w("row_set", n_row, alone=True)
                G.memset(ks[1][0][32:33, :].bitcast(F32), 1.0).then_inc(S["slot_const"], 1)
                w("slot_const", 1)
                for gi in range(NH * NP):
                    _, _, rows, _, n, _ = PAIRS[gi % NP]
                    whole, hi, lo = p_buffers(gi)
                    w("p", gi + 1)
                    if gi >= 3:
                        w("pv", gi - 2)
                    G.tensor_tensor(lo[0:rows, 0:n], whole[0:rows, 0:n], hi[0:rows, 0:n].bitcast(F32), ALU.subtract).then_inc(S["p_lo"], 1)
                sum_squares(osq[:, :], osqt[:, :], 4, "o_sq", "o_sum")
                sum_squares(msq[:, :], rs[:, :], 8, "xm_sq", "xm_sum")
                for m in range(8):
                    w("res_add", GROUPS * 8 + m + 1, alone=True)
                    save_x(m)
                    if m:
                        pool.wait_ge(S["sq"], L * 8 + 8 + m + 1)
                        if m > 1:
                            pool.wait_ge(S["sq_sum"], L * 7 + 7 + m - 1)
                        G.tensor_tensor(msq[:, :], msq[:, :], rs[:, :], ALU.add).then_inc(S["sq_sum"], 1)
            pool.wait_ge(S["x_out"], DEPTH * 128 + 128)
            pool.wait_ge(S["kpe_out"], DEPTH * 16)
            pool.wait_ge(S["kv_out"], DEPTH * 32)
            pool.wait_ge(S["small_out"], DEPTH * 32)


_OUTS = [("yT", (8, P, T)), ("ckv_out", (DEPTH, 2, P, TOK)), ("kpe_out", (DEPTH, ROPE, TOK)), ("h_out", (DEPTH, P, 4, 2)),
         ("conv_out", (DEPTH, P, 4, 2, CW - 1))]


def kernel(**inputs):
    import concourse.bacc as _bacc
    from concourse.bass_utils import run_bass_kernel_spmd as _run

    a = {k: np.asarray(v) for k, v in inputs.items()}
    f32 = np.float32

    tokens = np.concatenate([a["meta_tokens"], a["x_prompt"][0], a["x_sample"][0], np.zeros((2, DM), f32)], 0)
    arrays = {"xT": np.ascontiguousarray(tokens.T).reshape(8, P, T)}

    def block(w):
        k, m = w.shape
        return w.reshape(k // P, P, m).transpose(1, 0, 2).reshape(P, -1)

    wst = np.zeros((DEPTH * NB, P, 1024), f32)
    s0, s1, s2, s3 = QL, QL + KVL, QL + KVL + ROPE, QL + KVL + ROPE + LRU
    for l in range(DEPTH):
        def put(b, w):
            wst[l * NB + b, :, 0:w.shape[1]] = w

        w_in = a["w_in"][l]
        for c in range(4):
            put(B_XR[c], block(w_in[:, s2 + P * c:s2 + P * c + P]))
            put(B_GR[c], block(w_in[:, s3 + P * c:s3 + P * c + P]))
            gate = np.zeros((P, 2 * P), f32)
            for n, name in enumerate(("w_gate_a", "w_gate_x")):
                for i in range(2):
                    gate[64 * i:64 * i + 64, P * n + 64 * i:P * n + 64 * i + 64] = a[name][l, 2 * c + i]
            put(B_GATE[c], gate)
        for c in range(2):
            put(B_CKV[c], block(w_in[:, s0 + P * c:s0 + P * c + P]))
        put(B_KR, block(np.concatenate([w_in[:, s1:s2]] * 4, 1)))
        for c in range(6):
            put(B_CQ[c], block(w_in[:, P * c:P * c + P]))
        uq = a["w_uq"][l].reshape(QL, NH, NOPE + ROPE)
        nope, rot = uq[:, :, 0:NOPE].reshape(QL, -1), uq[:, :, NOPE:].reshape(QL, -1)
        for c in range(4):
            put(B_UQ + c, block(nope[:, P * c:P * c + P]))
        for c in range(2):
            put(B_UQ + 4 + c, block(rot[:, P * c:P * c + P]))
        ukv = a["w_ukv"][l].reshape(KVL, NH, NOPE + VD)
        put(B_UV, block(ukv[:, :, NOPE:].reshape(KVL, -1)))
        uk = ukv[:, :, 0:NOPE].reshape(KVL, -1)
        put(B_UK, np.concatenate([block(uk[:, P * j:P * j + P]) for j in range(4)], 1))
        wo = a["w_out"][l]
        for i, ms in enumerate(OY_TILES):
            put(B_OY + i, np.concatenate([block(wo[ATT:, P * m:P * m + P]) for m in ms], 1))
        for i in range(4):
            put(B_OO + i, np.concatenate([block(wo[0:ATT, P * m:P * m + P]) for m in (2 * i, 2 * i + 1)], 1))
        up, down = a["w_up"][l], a["w_down"][l]
        for q in range(GROUPS):
            for k in range(GT):
                f = GT * q + k
                put(B_MLP + 2 * GT * q + k, block(up[:, P * f:P * f + P]))
                put(B_MLP + 2 * GT * q + GT + k, block(down[1024 * q:1024 * q + 1024, P * k:P * k + P]))
    arrays["wst"] = wst

    def cols(v):
        return v.reshape(-1, P).T

    vec = np.zeros((DEPTH, P, NVEC), f32)
    for l in range(DEPTH):
        cw = a["conv_w"][l].reshape(CW, 4, P).transpose(2, 1, 0).reshape(P, 16)
        parts = [cols(a["norm_mix_g"][l]), cols(a["q_norm_g"][l]), cols(a["kv_norm_g"][l]), cw, cols(a["conv_b"][l]), cols(a["b_gate_a"][l]),
                 cols(a["b_gate_x"][l]), cols(a["lru_lambda"][l]), cols(a["attn_out_g"][l]), cols(a["lru_out_g"][l]), cols(a["norm_mlp_g"][l]),
                 cols(a["norm_mix_g"][min(l + 1, DEPTH - 1)])]
        vec[l] = np.concatenate(parts, 1)
    arrays["vec"] = vec
    arrays["fgain"] = np.ascontiguousarray(cols(a["final_norm_g"]))

    pos = np.concatenate([np.arange(-NMETA, SEQ), PAST + np.arange(DEC), np.zeros(2)]).astype(f32)
    inv = (f32(10000.0) ** (-np.arange(0, ROPE, 2, dtype=f32) / f32(ROPE))).astype(f32)
    ang = inv[:, None] * pos[None, :]
    cos, sin = np.cos(ang).astype(f32), np.sin(ang).astype(f32)
    arrays["ropeC"] = np.tile(np.concatenate([cos, cos], 0), (4, 1))
    arrays["ropeS"] = np.tile(np.concatenate([-sin, sin], 0), (4, 1))
    arrays["consts"] = np.stack([np.eye(P, dtype=f32), np.ones((P, P), f32)])
    arrays["past_ckv"] = np.ascontiguousarray(a["cache_ckv"][:, 0].transpose(0, 2, 1).reshape(DEPTH, 2, P, PAST).transpose(0, 2, 1, 3))
    arrays["past_kpe"] = np.ascontiguousarray(a["cache_kpe"][:, 0].transpose(0, 2, 1))
    arrays["h0"] = np.ascontiguousarray(a["state_lru_h"][:, 0].reshape(DEPTH, 4, P).transpose(0, 2, 1))
    arrays["conv0"] = np.ascontiguousarray(a["state_conv"][:, 0].reshape(DEPTH, CW - 1, 4, P).transpose(0, 3, 2, 1))

    nc = _bacc.Bacc("TRN2", target_bir_lowering=False, num_devices=1)
    args = [nc.dram_tensor(f"in_{n}", v.shape, F32, kind="ExternalInput").ap() for n, v in arrays.items()]
    args += [nc.dram_tensor(f"out_{n}", s, F32, kind="ExternalOutput").ap() for n, s in _OUTS]
    args += [nc.dram_tensor("x_scratch", (8, P, T), F32, kind="Internal").ap(), nc.dram_tensor("sum_scratch", (NH, TOK), F32, kind="Internal").ap()]
    trunk(nc, *args)
    res = _run(nc, [{f"in_{n}": v for n, v in arrays.items()}], core_ids=[0]).results[0]
    yT, ckv, kpe, hs, cv = (res[f"out_{n}"] for n, _ in _OUTS)

    y = yT.reshape(DM, T).T
    ckv = ckv.reshape(DEPTH, KVL, TOK).transpose(0, 2, 1)
    kpe = kpe.transpose(0, 2, 1)
    hs = hs.transpose(3, 0, 2, 1).reshape(2, DEPTH, 1, LRU)
    cv = cv.transpose(3, 0, 4, 2, 1).reshape(2, DEPTH, 1, CW - 1, LRU)
    p, s = slice(NMETA, STREAM), slice(STREAM, TOK)
    out = (y[None, p], y[None, s], ckv[:, None, p], kpe[:, None, p], hs[0], cv[0], ckv[:, None, s], kpe[:, None, s], hs[1], cv[1])
    return tuple(np.ascontiguousarray(v) for v in out)
```
